# Optimizing a Trainium2 kernel written in Bass

```python
import jax, jax.numpy as jnp
from jax import lax
import numpy as np

D_MODEL = 1024
BATCH = 1
SEQ = 1024
DEPTH = 1

N_META = 16
CHUNK = 64
N_PAD = CHUNK - N_META
EPS = 1e-6

GLA_HEADS = 4
GLA_DV = D_MODEL // 2 // GLA_HEADS
GLA_DK = GLA_DV // 2
GLA_GATE_RANK = 16
GLA_GATE_TAU = 16.0

RET_HEADS = 4
RET_DV = D_MODEL // 2 // RET_HEADS
RET_DK = RET_DV // 2
ROPE_BASE = 10000.0

IN_SPLITS = (
    GLA_HEADS * GLA_DK,
    GLA_HEADS * GLA_DK,
    GLA_HEADS * GLA_DV,
    GLA_HEADS * GLA_DV,
    GLA_GATE_RANK,
    RET_HEADS * RET_DK,
    RET_HEADS * RET_DK,
    RET_HEADS * RET_DV,
    RET_HEADS * RET_DV,
)
IN_WIDTH = sum(IN_SPLITS)
MIX_WIDTH = GLA_HEADS * GLA_DV + RET_HEADS * RET_DV

PEER_HEADS = 8
PEER_NKEYS = 128
PEER_NEXPERTS = PEER_NKEYS * PEER_NKEYS
PEER_DKEY = 256
PEER_TOPK = 16

kernel_name = "hybrid_gla_retnet_peer_meta"

def rmsnorm(x, g):
    xf = x.astype(jnp.float32)
    y = xf * lax.rsqrt(jnp.mean(xf * xf, axis=-1, keepdims=True) + EPS)
    return (y * g.astype(jnp.float32)).astype(x.dtype)

def to_chunks(t, n_heads, d):
    b, p, _ = t.shape
    return t.reshape(b, p // CHUNK, CHUNK, n_heads, d).transpose(0, 3, 1, 2, 4)

def from_chunks(t):
    b, h, n, c, d = t.shape
    return t.transpose(0, 2, 3, 1, 4).reshape(b, n * c, h * d)

def apply_rope(t, cos, sin):
    t1, t2 = jnp.split(t, 2, axis=-1)
    c = cos[None, :, None, :]
    s = sin[None, :, None, :]
    return jnp.concatenate([t1 * c - t2 * s, t1 * s + t2 * c], axis=-1)

def gla_chunked(q, k, v, log_a):
    bcum = jnp.cumsum(log_a, axis=-2)
    b_last = bcum[..., -1:, :]
    q_t = q * jnp.exp(bcum)
    k_t = k * jnp.exp(-bcum)
    causal = jnp.tril(jnp.ones((CHUNK, CHUNK), dtype=bool))
    att = jnp.einsum('bhnid,bhnjd->bhnij', q_t, k_t)
    att = jnp.where(causal, att, 0.0)
    o_intra = jnp.einsum('bhnij,bhnjv->bhniv', att, v)
    k_end = k * jnp.exp(b_last - bcum)
    chunk_kv = jnp.einsum('bhnjd,bhnjv->bhndv', k_end, v)
    chunk_decay = jnp.exp(b_last[..., 0, :])

    def step(state, inp):
        kv_n, a_n = inp
        return a_n[..., None] * state + kv_n, state

    b, h, n, c, dk = q.shape
    s0 = jnp.zeros((b, h, dk, v.shape[-1]), jnp.float32)
    _, s_prev = lax.scan(step, s0, (jnp.moveaxis(chunk_kv, 2, 0), jnp.moveaxis(chunk_decay, 2, 0)))
    s_prev = jnp.moveaxis(s_prev, 0, 2)
    o_inter = jnp.einsum('bhnid,bhndv->bhniv', q_t, s_prev)
    return o_intra + o_inter

def retention_chunked(q, k, v, log_gamma):
    idx = jnp.arange(CHUNK, dtype=jnp.float32)
    lg = log_gamma[:, None]
    diff = idx[:, None] - idx[None, :]
    dmat = jnp.where(diff >= 0, jnp.exp(lg[..., None] * jnp.maximum(diff, 0.0)), 0.0)
    att = jnp.einsum('bhnid,bhnjd->bhnij', q, k) * dmat[None, :, None]
    o_intra = jnp.einsum('bhnij,bhnjv->bhniv', att, v)
    xi = jnp.exp(lg * (idx + 1.0))
    zeta = jnp.exp(lg * (CHUNK - 1.0 - idx))
    chunk_kv = jnp.einsum('bhnjd,hj,bhnjv->bhndv', k, zeta, v)
    gamma_chunk = jnp.exp(log_gamma * CHUNK)[None, :, None, None]

    def step(state, kv_n):
        return gamma_chunk * state + kv_n, state

    b, h, n, c, dk = q.shape
    r0 = jnp.zeros((b, h, dk, v.shape[-1]), jnp.float32)
    _, r_prev = lax.scan(step, r0, jnp.moveaxis(chunk_kv, 2, 0))
    r_prev = jnp.moveaxis(r_prev, 0, 2)
    o_inter = jnp.einsum('bhnid,bhndv->bhniv', q, r_prev) * xi[None, :, None, :, None]
    return o_intra + o_inter

def head_rmsnorm(o, g):
    return o * lax.rsqrt(jnp.mean(o * o, axis=-1, keepdims=True) + EPS) * g

def head_layernorm(o, g, b):
    mu = jnp.mean(o, axis=-1, keepdims=True)
    var = jnp.mean(jnp.square(o - mu), axis=-1, keepdims=True)
    return (o - mu) * lax.rsqrt(var + EPS) * g + b

def token_mixers(xn, w_in, gate_w2, gate_b, gla_gain, ret_gain, ret_bias, w_out,
                 valid, cos, sin, log_gamma):
    f32 = jnp.float32
    split_points = np.cumsum(IN_SPLITS)[:-1].tolist()
    proj = xn @ w_in
    gq, gk, gv, gg, ga, rq, rk, rv, rg = jnp.split(proj, split_points, axis=-1)
    mask = valid[None, :, None]

    log_a = jax.nn.log_sigmoid((ga @ gate_w2 + gate_b).astype(f32)) / GLA_GATE_TAU
    q = to_chunks(gq.astype(f32) * (GLA_DK ** -0.5), GLA_HEADS, GLA_DK)
    k = to_chunks((gk * mask).astype(f32), GLA_HEADS, GLA_DK)
    v = to_chunks(gv.astype(f32), GLA_HEADS, GLA_DV)
    o_gla = gla_chunked(q, k, v, to_chunks(log_a, GLA_HEADS, GLA_DK))
    o_gla = from_chunks(head_rmsnorm(o_gla, gla_gain.astype(f32)))
    o_gla = o_gla * jax.nn.silu(gg.astype(f32))

    b, p, _ = xn.shape
    rq4 = apply_rope(rq.astype(f32).reshape(b, p, RET_HEADS, RET_DK), cos, sin)
    rk4 = apply_rope((rk * mask).astype(f32).reshape(b, p, RET_HEADS, RET_DK), cos, sin) * (RET_DK ** -0.5)
    q = to_chunks(rq4.reshape(b, p, -1), RET_HEADS, RET_DK)
    k = to_chunks(rk4.reshape(b, p, -1), RET_HEADS, RET_DK)
    v = to_chunks(rv.astype(f32), RET_HEADS, RET_DV)
    o_ret = retention_chunked(q, k, v, log_gamma)
    o_ret = from_chunks(head_layernorm(o_ret, ret_gain.astype(f32), ret_bias.astype(f32)))
    o_ret = o_ret * jax.nn.silu(rg.astype(f32))

    o = jnp.concatenate([o_gla, o_ret], axis=-1).astype(xn.dtype)
    return o @ w_out

def peer(xn, w_q, subkeys, u, v):
    b, p, d = xn.shape
    n_chunks = p // CHUNK
    xb = xn.reshape(b, n_chunks, CHUNK, d).transpose(1, 0, 2, 3).reshape(n_chunks, b * CHUNK, d)

    def block(xt):
        t = xt.shape[0]
        q = (xt @ w_q).reshape(t, PEER_HEADS, 2, PEER_DKEY // 2)
        s = jnp.einsum('thcd,hcnd->thcn', q, subkeys).astype(jnp.float32)
        s_top, i_top = lax.top_k(s, PEER_TOPK)
        cand = s_top[:, :, 0, :, None] + s_top[:, :, 1, None, :]
        cand_idx = i_top[:, :, 0, :, None] * PEER_NKEYS + i_top[:, :, 1, None, :]
        best, pos = lax.top_k(cand.reshape(t, PEER_HEADS, PEER_TOPK * PEER_TOPK), PEER_TOPK)
        idx = jnp.take_along_axis(cand_idx.reshape(t, PEER_HEADS, PEER_TOPK * PEER_TOPK), pos, axis=-1)
        g = jax.nn.softmax(best, axis=-1)
        u_sel = u[idx]
        act = jax.nn.gelu(jnp.einsum('td,thkd->thk', xt, u_sel).astype(jnp.float32), approximate=False)
        coef = (g * act).astype(xt.dtype)
        v_sel = v[idx]
        return jnp.einsum('thk,thkd->td', coef, v_sel)

    out = lax.map(block, xb)
    return out.reshape(n_chunks, b, CHUNK, d).transpose(1, 0, 2, 3).reshape(b, p, d)

def setup_inputs(seed: int = 0) -> dict:
    key = jax.random.key(seed)
    ks = jax.random.split(key, 16)
    f32 = jnp.float32
    nrm = lambda k, shape, scale: jax.random.normal(k, shape, f32) * scale
    return {
        "x": nrm(ks[0], (BATCH, SEQ, D_MODEL), 1.0),
        "meta_tokens": nrm(ks[1], (N_META, D_MODEL), 1.0),
        "norm1_gain": 1.0 + nrm(ks[2], (DEPTH, D_MODEL), 0.02),
        "w_in": nrm(ks[3], (DEPTH, D_MODEL, IN_WIDTH), D_MODEL ** -0.5),
        "gla_gate_w2": nrm(ks[4], (DEPTH, GLA_GATE_RANK, GLA_HEADS * GLA_DK), GLA_GATE_RANK ** -0.5),
        "gla_gate_b": nrm(ks[5], (DEPTH, GLA_HEADS * GLA_DK), 0.1),
        "gla_norm_gain": 1.0 + nrm(ks[6], (DEPTH, GLA_DV), 0.02),
        "ret_norm_gain": 1.0 + nrm(ks[7], (DEPTH, RET_DV), 0.02),
        "ret_norm_bias": nrm(ks[8], (DEPTH, RET_DV), 0.02),
        "w_out": nrm(ks[9], (DEPTH, MIX_WIDTH, D_MODEL), MIX_WIDTH ** -0.5),
        "norm2_gain": 1.0 + nrm(ks[10], (DEPTH, D_MODEL), 0.02),
        "peer_w_q": nrm(ks[11], (DEPTH, D_MODEL, PEER_HEADS * PEER_DKEY), D_MODEL ** -0.5),
        "peer_subkeys": nrm(ks[12], (DEPTH, PEER_HEADS, 2, PEER_NKEYS, PEER_DKEY // 2), (PEER_DKEY // 2) ** -0.5),
        "peer_u": nrm(ks[13], (DEPTH, PEER_NEXPERTS, D_MODEL), D_MODEL ** -0.5),
        "peer_v": nrm(ks[14], (DEPTH, PEER_NEXPERTS, D_MODEL), PEER_HEADS ** -0.5),
        "final_gain": 1.0 + nrm(ks[15], (D_MODEL,), 0.02),
    }

def reference(x, meta_tokens, norm1_gain, w_in, gla_gate_w2, gla_gate_b, gla_norm_gain,
              ret_norm_gain, ret_norm_bias, w_out, norm2_gain, peer_w_q, peer_subkeys,
              peer_u, peer_v, final_gain):
    b, s, d = x.shape
    p = s + CHUNK
    pad = jnp.zeros((b, N_PAD, d), x.dtype)
    meta = jnp.broadcast_to(meta_tokens.astype(x.dtype)[None], (b, N_META, d))
    h = jnp.concatenate([pad, meta, x], axis=1)

    pos = (jnp.arange(p) - N_PAD).astype(jnp.float32)
    valid = (pos >= 0).astype(x.dtype)
    inv_freq = ROPE_BASE ** (-jnp.arange(0, RET_DK, 2, dtype=jnp.float32) / RET_DK)
    ang = pos[:, None] * inv_freq[None, :]
    cos, sin = jnp.cos(ang), jnp.sin(ang)
    log_gamma = jnp.log(1.0 - jnp.power(2.0, -5.0 - jnp.arange(RET_HEADS, dtype=jnp.float32)))

    for l in range(DEPTH):
        h = h + token_mixers(rmsnorm(h, norm1_gain[l]), w_in[l], gla_gate_w2[l], gla_gate_b[l],
                             gla_norm_gain[l], ret_norm_gain[l], ret_norm_bias[l], w_out[l],
                             valid, cos, sin, log_gamma).astype(h.dtype)
        h = h + peer(rmsnorm(h, norm2_gain[l]), peer_w_q[l], peer_subkeys[l],
                     peer_u[l], peer_v[l]).astype(h.dtype)

    h = rmsnorm(h, final_gain)
    return h[:, CHUNK:]


_drawn_inputs = setup_inputs


def setup_inputs(seed=0):
    import zlib

    import numpy as np

    out = dict(_drawn_inputs(seed))
    spreads = {}
    factors = {'gla_norm_gain': 35.843,
     'ret_norm_gain': 35.453,
     'ret_norm_bias': 36.016,
     'final_gain': 23.584,
     'norm2_gain': 17.208}
    for name, (base, spread) in spreads.items():
        noise = np.random.default_rng([zlib.crc32(name.encode()), seed]).standard_normal(out[name].shape)
        drawn = base * np.exp(spread * noise) if base else spread * noise
        out[name] = __import__('jax').numpy.asarray(drawn.astype(out[name].dtype))
    for name, factor in factors.items():
        out[name] = (out[name] * factor).astype(out[name].dtype)
    return out
```

```python
import concourse.bass as bass
from concourse import mybir
from contextlib import ExitStack

F32 = mybir.dt.float32
U32 = mybir.dt.uint32
ALU = mybir.AluOpType
ACT = mybir.ActivationFunctionType
AX = mybir.AxisListType

P = 128
D = 1024
KC = D // P
HEADS = 4
DK, DV = 64, 128
PAIRS = HEADS // 2
CH = 64
SEQ, NMETA = 1024, 16
TILES = SEQ // P
BANK = 512
EPS = 1e-6
GQK, GV, GG, GA, RQK, RV, RG = 0, 512, 1024, 1536, 1552, 2064, 2576
RANK = 16
IN_WIDTH = 3088
PH, NK, TOPK = 8, 128, 16
SIDES = 2
HC = PH * SIDES
SLOTS = PH * TOPK
UR, VR, DR = 4, 8, 8
LOWEST = -3.4028235e38
C_ID, C_ONE, C_EPS, C_IOTA, C_END = 0, 128, 129, 130, 146
M_TRI, M_REV, M_MASK, M_DMAT, M_XI, M_ZETA, M_GAM, M_IND, M_END = 0, 128, 256, 384, 896, 1152, 1156, 1158, 1160
ROPE_W = 96


def mixer_phase(nc, block, io, shared, sem):
    h_all, cst = shared["h"], shared["cst"]
    ident = cst[:, C_ID:C_ID + P]
    with ExitStack() as ctx:
        def sb(name, shape, dt=F32):
            return ctx.enter_context(nc.sbuf_tensor(name, shape, dt))

        def ps(name):
            return ctx.enter_context(nc.psum_tensor(name, [P, BANK], F32))

        w_in = sb("w_in_sb", [P, KC, IN_WIDTH])
        mix = sb("mix_sb", [P, M_END])
        rope = sb("rope_sb", [P, TILES + 1, ROPE_W])
        gain1 = sb("gain1", [P, D])
        xn = sb("xn", [P, D])
        xT = sb("xT", [P, KC, P])
        junk = sb("junk", [P, D], mybir.dt.bfloat16)
        stat = sb("stat", [P, 4])
        gaT = sb("gaT", [RANK + 1, P])
        w2b = sb("w2b", [RANK + 1, HEADS * DK])
        absz = sb("absz", [P, 256])
        log_a = sb("log_a", [P, 256])
        decay = sb("decay", [P, 3, 256])
        a_last = sb("a_last", [P, PAIRS, 2])
        gqk = sb("gqk", [P, 512])
        gqkk = sb("gqkk", [P, 3, 256])
        gT = sb("gT", [P, PAIRS, P])
        gqs = sb("gqs", [P, PAIRS, 2, P])
        ropeA = sb("ropeA", [P, 512])
        rqk = sb("rqk", [P, 512])
        kz = sb("kz", [P, 256])
        rT = sb("rT", [P, 2 * PAIRS, P])
        rqx = sb("rqx", [P, PAIRS, P])
        att_g = sb("att_g", [P, HEADS, P])
        att_r = sb("att_r", [P, HEADS, P])
        v_g = sb("v_g", [P, 512])
        v_r = sb("v_r", [P, 512])
        gate = sb("gate", [P, D])
        S_prev = sb("S_prev", [P, PAIRS, 256])
        S_mid = sb("S_mid", [P, PAIRS, 256])
        R_prev = sb("R_prev", [P, PAIRS, 256])
        sq = sb("sq", [P, 512])
        sq2 = sb("sq2", [P, D])
        hstat = sb("hstat", [P, 32])
        hg = sb("hg", [P, 3, DV])

        o_sb = sb("o_sb", [P, 2, PAIRS, 2, DV])
        o_g = o_sb[:, 0].rearrange("p a e d -> p (a e d)")
        o_r = o_sb[:, 1].rearrange("p a e d -> p (a e d)")

        pa = [ps(f"pa{i}") for i in range(8)]
        pT = [pa[2], pa[3]]


        @block.sync
        def _(sp):
            sp.wait_ge(sem["pad_zeroed"], 1)
            sp.dma_start(h_all[P - NMETA:P, 0, :], io["meta_tokens"][:, :]).then_inc(sem["x0_in"], 16)
            sp.dma_start(gain1[:], io["norm1_gain"][0:1, :].to_broadcast([P, D])).then_inc(sem["gain1_in"], 16)
            sp.dma_start(cst[:], io["cst"][:, :]).then_inc(sem["cst_in"], 16)
            sp.dma_start(mix[:], io["mix"][:, :]).then_inc(sem["cst_in"], 16)
            sp.dma_start(rope[:], io["rope"][:, :, :]).then_inc(sem["rope_in"], 16)
            for k in range(KC):
                sp.dma_start(w_in[:, k, :], io["w_in"][0, P * k:P * (k + 1), :]).then_inc(sem["w_in_in"], 16)
            sp.dma_start(h_all[:, 1:TILES + 1, :],
                         io["x"][0].rearrange("(t p) d -> p t d", p=P)).then_inc(sem["x_in"], 16)

        @block.gpsimd
        def _(pool):
            pool.dma_start(w2b[0:RANK, :], io["gla_gate_w2"][0]).then_inc(sem["gate_in"], 16)
            pool.dma_start(w2b[RANK:RANK + 1, :], io["gla_gate_b"][:, :]).then_inc(sem["gate_in"], 16)
            for i, n in enumerate(("gla_norm_gain", "ret_norm_gain", "ret_norm_bias")):
                pool.dma_start(hg[:, i, :], io[n][0:1, :].to_broadcast([P, DV])).then_inc(sem["hg_in"], 16)

        @block.tensor
        def _(pe):
            def project(bank, w, src, col, width=BANK, k0=0):
                for k in range(KC):
                    last = nc.tensor.matmul(bank[:, 0:width], src[:, k, :], w[:, k, col:col + width],
                                            start=(k == 0), stop=(k == KC - 1))
                return last

            def transpose_rows(t, prev=True):
                pe.wait_ge(sem["xn"], t + 1)
                if prev:
                    pe.wait_ge(sem["S_new"], t - 1)
                for k in range(KC):
                    last = nc.tensor.transpose(pT[k // 4][:, P * (k % 4):P * (k % 4 + 1)],
                                               xn[:, P * k:P * (k + 1)], ident)
                    if k % 4 == 3:
                        last.then_inc(sem["xT_ps"], 1)

            def tile(t, prev=True, final=False):
                if not prev:
                    pe.wait_ge(sem["w_in_in"], 16 * KC)
                    pe.wait_ge(sem["xT"], 2)
                if prev:
                    pe.wait_ge(sem["decay_last"], t)
                for k in range(KC):
                    last = nc.tensor.matmul(pa[4][0:RANK, 0:P], w_in[:, k, GA:GA + RANK], xT[:, k, :],
                                            start=(k == 0), stop=(k == KC - 1))
                last.then_inc(sem["ga_ps"], 1)
                if prev:
                    pe.wait_ge(sem["gate_g"], t)
                project(pa[0], w_in, xT, GQK).then_inc(sem["gqk_ps"], 1)
                pe.wait_ge(sem["gaT"], t + 1)
                nc.tensor.matmul(pa[4][:, P:P + 256], gaT[:, :], w2b[:, :], start=True, stop=True).then_inc(sem["z_ps"], 1)
                if prev:
                    pe.wait_ge(sem["gate_r"], t)
                project(pa[1], w_in, xT, RQK).then_inc(sem["rqk_ps"], 1)
                pe.wait_ge(sem["gqk"], t + 1)
                project(pa[0], w_in, xT, GV).then_inc(sem["gv_ps"], 1)
                pe.wait_ge(sem["log_a"], t + 1)
                if prev:
                    pe.wait_ge(sem["R_new"], t)
                nc.tensor.matmul(pa[5][:, 0:256], mix[:, M_TRI:M_TRI + P], log_a[:], start=True, stop=True)
                nc.tensor.matmul(pa[5][:, 256:512], mix[:, M_REV:M_REV + P], log_a[:], start=True, stop=True)
                for p in range(PAIRS):
                    last = nc.tensor.matmul(pa[4][:, 384 + 2 * p:386 + 2 * p], log_a[:, P * p:P * (p + 1)],
                                            mix[:, M_IND:M_IND + 2], start=True, stop=True)
                last.then_inc(sem["cum_ps"], 1)
                pe.wait_ge(sem["rope"], t + 1)
                project(pa[1], w_in, xT, RV).then_inc(sem["rv_ps"], 1)
                pe.wait_ge(sem["gv"], t + 1)
                project(pa[0], w_in, xT, GG).then_inc(sem["gg_ps"], 1)
                pe.wait_ge(sem["gqkk"], t + 1)
                if prev:
                    pe.wait_ge(sem["o"], 2 * t)
                for i in range(4):
                    last = nc.tensor.transpose(pa[6][:, P * i:P * (i + 1)],
                                               gqkk[:, i // 2, P * (i % 2):P * (i % 2 + 1)], ident)
                last.then_inc(sem["gT_ps"], 1)
                for i in range(4):
                    last = nc.tensor.transpose(pa[7][:, P * i:P * (i + 1)], rqk[:, P * i:P * (i + 1)], ident)
                last.then_inc(sem["rT_ps"], 1)
                pe.wait_ge(sem["rv"], t + 1)
                project(pa[1], w_in, xT, RG).then_inc(sem["rg_ps"], 1)
                if not final:
                    transpose_rows(t + 1, prev)
                pe.wait_ge(sem["gqs"], t + 1)
                pe.wait_ge(sem["gT"], t + 1)
                pe.wait_ge(sem["rT"], t + 1)
                for h in range(HEADS):
                    rows = slice(DK * (h % 2), DK * (h % 2) + DK)
                    for c in range(2):
                        nc.tensor.matmul(pa[6 + h % 2][:, P * (h // 2) + CH * c:P * (h // 2) + CH * (c + 1)], gT[rows, h // 2, :],
                                         gqs[rows, h // 2, c, CH * c:CH * (c + 1)], start=True, stop=True)
                for h in range(HEADS):
                    rows = slice(DK * (h % 2), DK * (h % 2) + DK)
                    last = nc.tensor.matmul(pa[6 + h % 2][:, 256 + P * (h // 2):256 + P * (h // 2 + 1)], rT[rows, 2 + h // 2, :],
                                            rT[rows, h // 2, :], start=True, stop=True)
                    if h >= 2:
                        last.then_inc(sem["att_ps"], 1)
                if not final:
                    pe.wait_ge(sem["xT"], 2 * t + 4)
                for c in range(2):
                    for p in range(PAIRS):
                        rows = slice(CH * c, CH * (c + 1))
                        last = nc.tensor.matmul(pT[c][:, 256 * p:256 * (p + 1)], gqkk[rows, 2, P * p:P * (p + 1)],
                                                v_g[rows, 256 * p:256 * (p + 1)], start=True, stop=True)
                    last.then_inc(sem["kv_g_ps"], 1)
                for p in range(PAIRS):
                    last = nc.tensor.matmul(pa[5][:, 256 * p:256 * (p + 1)], kz[:, P * p:P * (p + 1)],
                                            v_r[:, 256 * p:256 * (p + 1)], start=True, stop=True)
                last.then_inc(sem["kv_r_ps"], 1)
                pe.wait_ge(sem["att"], t + 1)
                pe.wait_ge(sem["rqx"], t + 1)
                pe.wait_ge(sem["S_mid"], t + 1)
                if not prev:
                    pe.wait_ge(sem["state0"], 1)
                for h in range(HEADS):
                    rows = slice(DK * (h % 2), DK * (h % 2) + DK)
                    vc = slice(P * (h % 2), P * (h % 2) + P)
                    o = pa[6 + h % 2][:, P * (h // 2):P * (h // 2 + 1)]
                    nc.tensor.matmul(o, att_g[:, h, :], v_g[:, P * h:P * (h + 1)], start=True, stop=False)
                    nc.tensor.matmul(o, gqs[rows, h // 2, 0, :], S_prev[rows, h // 2, vc], start=False, stop=False)
                    nc.tensor.matmul(o, gqs[rows, h // 2, 1, :], S_mid[rows, h // 2, vc], start=False, stop=True)
                for h in range(HEADS):
                    rows = slice(DK * (h % 2), DK * (h % 2) + DK)
                    vc = slice(P * (h % 2), P * (h % 2) + P)
                    o = pa[6 + h % 2][:, 256 + P * (h // 2):256 + P * (h // 2 + 1)]
                    nc.tensor.matmul(o, att_r[:, h, :], v_r[:, P * h:P * (h + 1)], start=True, stop=False)
                    last = nc.tensor.matmul(o, rqx[rows, h // 2, :], R_prev[rows, h // 2, vc], start=False, stop=True)
                    if h >= 2:
                        last.then_inc(sem["o_ps"], 1)

            pe.wait_ge(sem["cst_in"], 32)
            pe.wait_ge(sem["gate_in"], 32)
            transpose_rows(0, prev=False)
            tile(0, prev=False)
            with pe.Fori(1, TILES) as t:
                tile(t)
            tile(TILES, final=True)

        @block.scalar
        def _(act):
            A = nc.scalar.activation

            def row_root(t):
                A(junk[:], h_all[:, bass.ds(t, 1), :], ACT.Square, accum_out=stat[:, 0:1]).then_inc(sem["ss"], 1)
                act.wait_ge(sem["ss"], t + 1)
                A(stat[:, 1:2], stat[:, 0:1], ACT.Sqrt, bias=cst[:, C_EPS:C_EPS + 1], scale=1.0 / D).then_inc(sem["rms"], 1)

            def copy_rows(t):
                for i in range(2):
                    act.wait_ge(sem["xT_ps"], 2 * t + i + 1)
                    A(xT[:, 4 * i:4 * i + 4, :], pT[i][:], ACT.Copy).then_inc(sem["xT"], 1)

            def tile(t, prev=True, final=False):
                if not final:
                    row_root(t + 1)
                act.wait_ge(sem["ga_ps"], t + 1)
                A(gaT[0:RANK, :], pa[4][0:RANK, 0:P], ACT.Copy).then_inc(sem["gaT"], 1)
                act.wait_ge(sem["gqk_ps"], t + 1)
                A(gqk[:], pa[0][:], ACT.Copy).then_inc(sem["gqk"], 1)
                act.wait_ge(sem["z_ps"], t + 1)
                A(absz[:], pa[4][:, P:P + 256], ACT.Abs).then_inc(sem["absz"], 1)
                act.wait_ge(sem["absz"], 3 * t + 1)
                A(absz[:], absz[:], ACT.Exp, scale=-1.0).then_inc(sem["absz"], 1)
                act.wait_ge(sem["absz"], 3 * t + 2)
                A(absz[:], absz[:], ACT.Ln, bias=cst[:, C_ONE:C_ONE + 1]).then_inc(sem["absz"], 1)
                act.wait_ge(sem["gv_ps"], t + 1)
                A(v_g[:], pa[0][:], ACT.Copy).then_inc(sem["gv"], 1)
                act.wait_ge(sem["cum_ps"], t + 1)
                A(a_last[:], pa[4][:, 384:388], ACT.Exp).then_inc(sem["decay_last"], 1)
                A(decay[:, 0, :], pa[5][:, 0:256], ACT.Exp)
                A(decay[:, 1, :], pa[5][:, 0:256], ACT.Exp, scale=-1.0)
                A(decay[:, 2, :], pa[5][:, 256:512], ACT.Exp).then_inc(sem["decay"], 1)
                act.wait_ge(sem["rv_ps"], t + 1)
                A(v_r[:], pa[1][:], ACT.Copy).then_inc(sem["rv"], 1)
                act.wait_ge(sem["gg_ps"], t + 1)
                A(gate[:, 0:512], pa[0][:], ACT.Silu).then_inc(sem["gate_g"], 1)
                act.wait_ge(sem["gqs"], t + 1)
                A(gT[:], pa[6][:, 256:512], ACT.Copy).then_inc(sem["gT"], 1)
                act.wait_ge(sem["rT_ps"], t + 1)
                A(rT[:], pa[7][:], ACT.Copy).then_inc(sem["rT"], 1)
                act.wait_ge(sem["rg_ps"], t + 1)
                A(gate[:, 512:1024], pa[1][:], ACT.Silu).then_inc(sem["gate_r"], 1)
                if not final:
                    copy_rows(t + 1)
                for e in range(2):
                    act.wait_ge(sem["o_ps"], 2 * t + e + 1)
                    A(o_sb[:, :, :, e, :], pa[6 + e][:].rearrange("p (g a d) -> p g a d", g=2, a=PAIRS), ACT.Copy).then_inc(sem["o"], 1)
                act.wait_ge(sem["o"], 2 * t + 2)
                A(sq[:], o_g, ACT.Square).then_inc(sem["sq_g"], 1)
                act.wait_ge(sem["centred"], t + 1)
                A(sq2[:, 512:1024], sq2[:, 0:512], ACT.Square).then_inc(sem["sq_r"], 1)
                act.wait_ge(sem["hss"], t + 1)
                A(hstat[:, 8:16], hstat[:, 0:8], ACT.Sqrt, bias=cst[:, C_EPS:C_EPS + 1], scale=1.0 / DV).then_inc(sem["hroot"], 1)

            act.wait_ge(sem["cst_in"], 32)
            act.wait_ge(sem["x0_in"], 16)
            row_root(0)
            copy_rows(0)
            act.wait_ge(sem["x_in"], 16)
            tile(0, prev=False)
            with act.Fori(1, TILES) as t:
                tile(t)
            tile(TILES, final=True)

        @block.vector
        def _(dve):
            V = nc.vector

            def heads(ap, n=DV):
                return ap.rearrange("p (h d) -> p h d", d=n)

            def normed(t, prev=True):
                dve.wait_ge(sem["rms"], t + 1)
                V.reciprocal(stat[:, 2:3], stat[:, 1:2]).then_inc(sem["rstd"], 1)
                dve.wait_ge(sem["rstd"], t + 1)
                if prev:
                    dve.wait_ge(sem["xT_ps"], 2 * t)
                V.scalar_tensor_tensor(xn[:], h_all[:, bass.ds(t, 1), :].rearrange("p o d -> p (o d)"), stat[:, 2:3],
                                       gain1[:], ALU.mult, ALU.mult).then_inc(sem["xn"], 1)

            def tile(t, prev=True, final=False):
                dve.wait_ge(sem["absz"], 3 * t + 3)
                if prev:
                    dve.wait_ge(sem["cum_ps"], t)
                V.scalar_tensor_tensor(log_a[:], pa[4][:, P:P + 256], 0.0, absz[:], ALU.min, ALU.subtract).then_inc(sem["log_a"], 1)
                dve.wait_ge(sem["rqk_ps"], t + 1)
                src = pa[1][:].rearrange("p (n s c) -> p n s c", s=2, c=DK // 2)
                tmp = ropeA[:].rearrange("p (n s c) -> p n s c", s=2, c=DK // 2)
                dst = rqk[:].rearrange("p (n s c) -> p n s c", s=2, c=DK // 2)
                rt = rope[:, bass.ds(t, 1), :]
                cos = rt[:, :, 0:32].to_broadcast([P, 8, 32])
                for s in range(2):
                    V.tensor_tensor(dst[:, :, s, :], src[:, :, s, :], cos, ALU.mult)
                for s in range(2):
                    sin = rt[:, :, 32 + 32 * s:64 + 32 * s].to_broadcast([P, 8, 32])
                    last = V.tensor_tensor(tmp[:, :, s, :], src[:, :, 1 - s, :], sin, ALU.mult)
                last.then_inc(sem["rope"], 1)
                dve.wait_ge(sem["rope"], t + 1)
                V.tensor_tensor(rqk[:], rqk[:], ropeA[:], ALU.add).then_inc(sem["roped"], 1)
                dve.wait_ge(sem["roped"], t + 1)
                zeta = mix[:, M_ZETA:M_ZETA + HEADS].unsqueeze(2).to_broadcast([P, HEADS, DK])
                V.tensor_tensor(heads(kz[:], DK), heads(rqk[:, 256:512], DK), zeta, ALU.mult).then_inc(sem["kz"], 1)
                dve.wait_ge(sem["decay"], t + 1)
                dve.wait_ge(sem["gqk"], t + 1)
                V.scalar_tensor_tensor(gqkk[:, 0, :], gqk[:, 0:256], DK ** -0.5, decay[:, 0, :], ALU.mult, ALU.mult)
                V.tensor_tensor(gqkk[:, 1, :], gqk[:, 256:512], decay[:, 1, :], ALU.mult)
                V.tensor_tensor(gqkk[:, 2, :], gqk[:, 256:512], decay[:, 2, :], ALU.mult).then_inc(sem["gqkk"], 1)
                if not final:
                    normed(t + 1)
                dve.wait_ge(sem["gT_ps"], t + 1)
                for c in range(2):
                    cs = slice(CH * c, CH * (c + 1))
                    last = V.tensor_copy(gqs[:, :, c, cs], pa[6][:, 0:256].rearrange("p (a i) -> p a i", i=P)[:, :, cs])
                last.then_inc(sem["gqs"], 1)
                dve.wait_ge(sem["rT"], t + 1)
                V.tensor_tensor(rqx[:], rT[:, 0:PAIRS, :],
                                mix[:, M_XI:M_XI + 256].rearrange("p (a i) -> p a i", i=P), ALU.mult).then_inc(sem["rqx"], 1)
                mask = mix[:, M_MASK:M_MASK + P].bitcast(U32).unsqueeze(1).to_broadcast([P, PAIRS, P])
                dmat = mix[:, M_DMAT:M_DMAT + 512].rearrange("p (a e i) -> p a e i", e=2, i=P)
                for e in range(2):
                    dve.wait_ge(sem["att_ps"], 2 * t + e + 1)
                    dve.nop(nofuse=True)
                    scores = pa[6 + e][:].rearrange("p (n i) -> p n i", i=P)
                    V.copy_predicated(att_g[:].rearrange("p (a e) i -> p a e i", e=2)[:, :, e, :], mask, scores[:, 0:2, :])
                    last = V.tensor_tensor(att_r[:].rearrange("p (a e) i -> p a e i", e=2)[:, :, e, :], scores[:, 2:4, :],
                                           dmat[:, :, e, :], ALU.mult)
                last.then_inc(sem["att"], 1)
                dve.wait_ge(sem["kv_g_ps"], 2 * t + 1)
                dve.wait_ge(sem["decay_last"], t + 1)
                for p in range(PAIRS):
                    last = V.scalar_tensor_tensor(S_mid[:, p, :], S_prev[:, p, :], a_last[:, p, 0:1],
                                                  pT[0][:, 256 * p:256 * (p + 1)], ALU.mult, ALU.add)
                last.then_inc(sem["S_mid"], 1)
                dve.wait_ge(sem["o_ps"], 2 * t + 2)
                dve.wait_ge(sem["kv_g_ps"], 2 * t + 2)
                dve.wait_ge(sem["S_mid"], t + 1)
                for p in range(PAIRS):
                    last = V.scalar_tensor_tensor(S_prev[:, p, :], S_mid[:, p, :], a_last[:, p, 1:2],
                                                  pT[1][:, 256 * p:256 * (p + 1)], ALU.mult, ALU.add)
                last.then_inc(sem["S_new"], 1)
                dve.wait_ge(sem["kv_r_ps"], t + 1)
                for p in range(PAIRS):
                    last = V.scalar_tensor_tensor(R_prev[:, p, :], R_prev[:, p, :], mix[:, M_GAM + p:M_GAM + p + 1],
                                                  pa[5][:, 256 * p:256 * (p + 1)], ALU.mult, ALU.add)
                last.then_inc(sem["R_new"], 1)
                dve.wait_ge(sem["o"], 2 * t + 2)
                V.tensor_reduce(hstat[:, 24:28], heads(o_r), AX.X, ALU.add).then_inc(sem["hmean"], 1)
                dve.wait_ge(sem["hmean"], 2 * t + 1)
                V.tensor_scalar(hstat[:, 28:32], hstat[:, 24:28], 1.0 / DV, None, ALU.mult).then_inc(sem["hmean"], 1)
                dve.wait_ge(sem["hmean"], 2 * t + 2)
                V.tensor_tensor(heads(sq2[:, 0:512]), heads(o_r),
                                hstat[:, 28:32].unsqueeze(2).to_broadcast([P, HEADS, DV]), ALU.subtract).then_inc(sem["centred"], 1)
                dve.wait_ge(sem["sq_g"], t + 1)
                V.tensor_reduce(hstat[:, 0:4], heads(sq[:]), AX.X, ALU.add)
                dve.wait_ge(sem["sq_r"], t + 1)
                V.tensor_reduce(hstat[:, 4:8], heads(sq2[:, 512:1024]), AX.X, ALU.add).then_inc(sem["hss"], 1)
                dve.wait_ge(sem["hroot"], t + 1)
                V.reciprocal(hstat[:, 16:24], hstat[:, 8:16]).then_inc(sem["hrstd"], 1)
                dve.wait_ge(sem["hrstd"], t + 1)
                mixed = h_all[:, bass.ds(t, 1), :].rearrange("p o d -> p (o d)")
                rs = hstat[:, 16:24].unsqueeze(2)
                V.tensor_tensor(heads(mixed[:, 0:512]), heads(o_g), rs[:, 0:4, :].to_broadcast([P, HEADS, DV]), ALU.mult)\
                 .then_inc(sem["norm_g"], 1)
                V.tensor_tensor(heads(mixed[:, 512:1024]), heads(sq2[:, 0:512]), rs[:, 4:8, :].to_broadcast([P, HEADS, DV]), ALU.mult)\
                 .then_inc(sem["norm_r"], 1)
                dve.wait_ge(sem["norm_r"], t + 1)
                V.tensor_tensor(heads(mixed[:, 0:512]), heads(mixed[:, 0:512]), hg[:, 0:1, :].to_broadcast([P, HEADS, DV]), ALU.mult)
                V.tensor_tensor(heads(mixed[:, 512:1024]), heads(mixed[:, 512:1024]), hg[:, 1:2, :].to_broadcast([P, HEADS, DV]), ALU.mult)\
                 .then_inc(sem["scaled"], 1)
                dve.wait_ge(sem["scaled"], 2 * t + 1)
                V.tensor_tensor(heads(mixed[:, 512:1024]), heads(mixed[:, 512:1024]), hg[:, 2:3, :].to_broadcast([P, HEADS, DV]), ALU.add)\
                 .then_inc(sem["scaled"], 1)
                dve.wait_ge(sem["scaled"], 2 * t + 2)
                dve.wait_ge(sem["gate_r"], t + 1)
                V.tensor_tensor(mixed, mixed, gate[:], ALU.mult).then_inc(sem["mixed"], 1)

            V.memset(h_all[:, 0, :], 0.0).then_inc(sem["pad_zeroed"], 1)
            V.memset(gaT[:], 1.0)
            V.memset(gqs[:], 0.0)
            V.memset(att_g[:], 0.0)
            V.memset(S_prev[:], 0.0)
            V.memset(R_prev[:], 0.0).then_inc(sem["state0"], 1)
            dve.wait_ge(sem["gain1_in"], 16)
            dve.wait_ge(sem["cst_in"], 32)
            dve.wait_ge(sem["hg_in"], 48)
            dve.wait_ge(sem["rope_in"], 16)
            dve.wait_ge(sem["state0"], 1)
            normed(0, prev=False)
            tile(0, prev=False)
            with dve.Fori(1, TILES) as t:
                tile(t)
            tile(TILES, final=True)


class Steps:

    def __init__(self, sem, per_tile, tile):
        self.sem, self.per_tile, self.base, self.n = sem, per_tile, tile * per_tile, 0

    def done(self, instruction):
        self.n += 1
        instruction.then_inc(self.sem, 1)

    def wait(self, engine):
        engine.wait_ge(self.sem, self.base + self.n)
        engine.nop(nofuse=True)


ROUTE_AT = {6: 0, 10: 1, 16: 2, 22: 3, 28: 4, 34: 5}
ROUTE_STEPS = 34


def peer_phase(nc, block, io, out, shared, sem):
    h_all, cst = shared["h"], shared["cst"]
    ident = cst[:, C_ID:C_ID + P]
    with ExitStack() as ctx:
        def sb(name, shape, dt=F32):
            return ctx.enter_context(nc.sbuf_tensor(name, shape, dt))

        def ps(name):
            return ctx.enter_context(nc.psum_tensor(name, [P, BANK], F32))

        w_q = sb("w_q", [P, KC, HC * P])
        skT = sb("skT", [P, HC, NK])
        work = sb("work", [P, KC * D])
        vrow = sb("vrow", [P, VR, D])
        diag = sb("diag", [P, DR, P])
        gain2 = sb("gain2", [P, D])
        gainf = sb("gainf", [P, D])
        xn_next = sb("xn_next", [P, D])
        xn_cur = sb("xn_cur", [P, D])
        xT = sb("xT_b", [P, KC, P])
        top = sb("top", [P, HC, TOPK])
        topi = sb("topi", [P, HC, TOPK], U32)
        topf = sb("topf", [P, HC, TOPK])
        best = sb("best", [P, PH, TOPK])
        pos = sb("pos", [P, SLOTS], U32)
        idx_next = sb("idx_next", [P, SLOTS], U32)
        idx_cur = sb("idx_cur", [P, SLOTS], U32)
        ex = sb("ex", [P, PH, TOPK])
        soft = sb("soft", [P, 16])
        g_next = sb("g_next", [P, SLOTS])
        g_cur = sb("g_cur", [P, SLOTS])
        dots = sb("dots", [P, SLOTS])
        acts = sb("acts", [P, SLOTS])
        coef = sb("coef", [P, SLOTS])
        cred = sb("cred", [P, 2])
        stat = sb("stat_b", [P, 8])

        w_out = work[:].rearrange("p (k n) -> p k n", n=D)
        urow = work[:, 0:UR * D].rearrange("p (r d) -> p r d", d=D)
        s_buf = work[:, 4096:6144]
        cand = work[:, 6144:8192]
        pos2 = cand[:, 0:256].bitcast(U32).rearrange("p (c n) -> p c n", c=2)
        posf = cand[:, 256:512].rearrange("p (c n) -> p c n", c=2)
        key = cand[:, 512:768].rearrange("p (c n) -> p c n", c=2)
        junk = h_all[:, 0, :]
        x_in = vrow
        sk_raw = [xn_cur[:], junk]
        o_ps = [ps("o_ps0"), ps("o_ps1")]
        x_ps = [ps("x_ps0"), ps("x_ps1")]
        q_ps = [ps("q_ps0"), ps("q_ps1")]
        s_ps = [ps("s_ps0"), ps("s_ps1")]
        qT = cand.rearrange("p (n i) -> p n i", i=P)

        def row(t):
            return h_all[:, bass.ds(t + 1, 1), :].rearrange("p o d -> p (o d)")

        @block.sync
        def _(sp):
            sp.dma_start(w_out, io["w_out"][0].rearrange("(k p) n -> p k n", p=P)).then_inc(sem["w_out_in"], 16)
            sp.dma_start(x_in[:], io["x"][0].rearrange("(t p) d -> p t d", p=P)).then_inc(sem["x_again"], 16)
            for i, half in enumerate(sk_raw):
                sp.dma_start(half.rearrange("p (n d) -> p n d", d=P),
                             io["peer_subkeys"][0].rearrange("h c n d -> n (h c) d")[:, 8 * i:8 * i + 8, :])\
                    .then_inc(sem["sk_in"], 16)
            sp.dma_start(gain2[:], io["norm2_gain"][0:1, :].to_broadcast([P, D])).then_inc(sem["gain2_in"], 16)
            sp.dma_start(gainf[:], io["final_gain"].rearrange("(a d) -> a d", a=1).to_broadcast([P, D])).then_inc(sem["gain2_in"], 16)
            for k in range(KC):
                sp.dma_start(w_q[:, k, :], io["peer_w_q"][0, P * k:P * (k + 1), :]).then_inc(sem["w_q_in"], 16)
            with sp.Fori(0, TILES) as t:
                sp.wait_ge(sem["y"], t + 1)
                sp.dma_start(out[0].rearrange("(t p) d -> p t d", p=P)[:, bass.ds(t, 1), :],
                             h_all[:, bass.ds(t + 1, 1), :]).then_inc(sem["stored"], 16)
            sp.wait_ge(sem["stored"], 16 * TILES)

        @block.gpsimd
        def _(pool):
            def gather(table, ring, n, size, free, landed, t):
                pool.wait_ge(free, t * SLOTS + n + 1)
                pool.nop(nofuse=True)
                pool.indirect_dma_start(out=ring[:, n % size, :], out_offset=None, in_=table,
                                        in_offset=bass.IndirectOffsetOnAxis(ap=idx_cur[:, n:n + 1], axis=0))\
                    .then_inc(landed[n % size], 16)

            pool.tensor_copy(xn_next[:], row(0)).then_inc(sem["mixed_at"], 1)
            with pool.Fori(1, TILES) as t:
                pool.wait_ge(sem["oT_ps"], 2 * t)
                pool.nop(nofuse=True)
                pool.tensor_copy(xn_next[:], row(t)).then_inc(sem["mixed_at"], 1)
            def stage(t, h, count):
                cols = slice(TOPK * h, TOPK * (h + 1))
                pool.tensor_copy(idx_cur[:, cols], idx_next[:, cols]).then_inc(sem["staged"], 1)
                pool.wait_ge(sem["staged"], count + 1)

            def gather_u(t, n):
                gather(io["peer_u"][0], urow, n, UR, sem["u_free"], sem["u_in"], t)

            def tile(t, last=False):
                for h in range(PH):
                    ahead = (t, h + 1) if h < PH - 1 else (t + 1, 0)
                    if h == PH - 1 and not last:
                        pool.wait_ge(sem["idx"], t + 2)
                        pool.nop(nofuse=True)
                    if not (h == PH - 1 and last):
                        stage(*ahead, PH * t + h + 1)
                    for k in range(TOPK):
                        if not (h == PH - 1 and last):
                            gather_u(ahead[0], TOPK * ahead[1] + k)
                        gather(io["peer_v"][0], vrow, TOPK * h + k, VR, sem["v_free"], sem["v_in"], t)

            pool.wait_ge(sem["idx"], 1)
            stage(0, 0, 0)
            for k in range(TOPK):
                gather_u(0, k)
            with pool.Fori(0, TILES - 1) as t:
                tile(t)
            tile(TILES - 1, last=True)

        @block.tensor
        def _(pe):
            def route(T, part, first=False):
                if part == 0:
                    pe.wait_ge(sem["xn2"], T + 1)
                    for k in range(KC):
                        last = nc.tensor.transpose(x_ps[k // 4][:, P * (k % 4):P * (k % 4 + 1)],
                                                   xn_next[:, P * k:P * (k + 1)], ident)
                        if k % 4 == 3:
                            last.then_inc(sem["x2T_ps"], 1)
                if 1 <= part <= 4:
                    g = part - 1
                    if g == 0:
                        pe.wait_ge(sem["x2T"], 2 * T + 2)
                        if first:
                            pe.wait_ge(sem["w_q_in"], 16 * KC)
                    if g >= 2:
                        pe.wait_ge(sem["qT"], 4 * T + g - 1)
                    for n in range(4 * g, 4 * g + 4):
                        for k in range(KC):
                            last = nc.tensor.matmul(q_ps[g % 2][:, P * (n % 4):P * (n % 4 + 1)],
                                                    w_q[:, k, P * n:P * (n + 1)], xT[:, k, :],
                                                    start=(k == 0), stop=(k == KC - 1))
                    last.then_inc(sem["q_ps"], 1)
                if part >= 2:
                    g = part - 2
                    pe.wait_ge(sem["qT"], 4 * T + g + 1)
                    if g >= 2:
                        pe.wait_ge(sem["s"], 4 * T + g - 1)
                    for n in range(4 * g, 4 * g + 4):
                        last = nc.tensor.matmul(s_ps[g % 2][:, P * (n % 4):P * (n % 4 + 1)],
                                                qT[:, n, :], skT[:, n, :], start=True, stop=True)
                    last.then_inc(sem["s_ps"], 1)

            def tile(t, first=False, last=False):
                if not first:
                    pe.wait_ge(sem["summed"], 2 * t)
                for n in range(SLOTS):
                    if n in ROUTE_AT and not last:
                        route(t + 1, ROUTE_AT[n])
                    pe.wait_ge(sem["v_in"][n % VR], 16 * (t * (SLOTS // VR) + n // VR + 1))
                    pe.wait_ge(sem["diag"], t * SLOTS + n + 1)
                    for i in range(2):
                        product = nc.tensor.matmul(o_ps[i][:], diag[:, n % DR, :], vrow[:, n % VR, BANK * i:BANK * (i + 1)],
                                                   start=(n == 0), stop=(n == SLOTS - 1))
                    product.then_inc(sem["v_free"], 1)

            def project_out(t, first=False):
                pe.wait_ge(sem["mixed_at"], t + 1)
                for k in range(KC):
                    last = nc.tensor.transpose(x_ps[k // 4][:, P * (k % 4):P * (k % 4 + 1)],
                                               xn_next[:, P * k:P * (k + 1)], ident)
                    if k % 4 == 3:
                        last.then_inc(sem["oT_ps"], 1)
                pe.wait_ge(sem["oT"], 2 * t + 2)
                for i in range(2):
                    if not first:
                        pe.wait_ge(sem["h"], 2 * t + i - 1)
                    for k in range(KC):
                        last = nc.tensor.matmul(o_ps[i][:], xT[:, k, :], w_out[:, k, BANK * i:BANK * (i + 1)],
                                                start=(k == 0), stop=(k == KC - 1))
                    last.then_inc(sem["out_ps"], 1)

            pe.wait_ge(sem["w_out_in"], 16)
            project_out(0, first=True)
            with pe.Fori(1, TILES) as t:
                project_out(t)
            pe.wait_ge(sem["sk_in"], 32)
            for g, bank in enumerate(q_ps + s_ps):
                for n in range(4):
                    last = nc.tensor.transpose(bank[:, P * n:P * (n + 1)],
                                               sk_raw[g // 2][:, P * (4 * (g % 2) + n):P * (4 * (g % 2) + n + 1)], ident)
                last.then_inc(sem["skT_ps"], 1)
            pe.wait_ge(sem["skT"], 4)
            for part in range(6):
                route(0, part, first=True)
            tile(0, first=True)
            with pe.Fori(1, TILES - 1) as t:
                tile(t)
            tile(TILES - 1, last=True)

        @block.scalar
        def _(act):
            A = nc.scalar.activation

            def row_root(T):
                A(xT[:].rearrange("p k i -> p (k i)"), row(T), ACT.Square, accum_out=stat[:, 0:1]).then_inc(sem["ss2"], 1)
                act.wait_ge(sem["ss2"], T + 1)
                A(stat[:, 1:2], stat[:, 0:1], ACT.Sqrt, bias=cst[:, C_EPS:C_EPS + 1], scale=1.0 / D).then_inc(sem["rms2"], 1)

            def route(T, part, first=False):
                if part == 0:
                    for i in range(2):
                        act.wait_ge(sem["x2T_ps"], 2 * T + i + 1)
                        A(xT[:, 4 * i:4 * i + 4, :], x_ps[i][:], ACT.Copy).then_inc(sem["x2T"], 1)
                if 1 <= part <= 4:
                    g = part - 1
                    act.wait_ge(sem["q_ps"], 4 * T + g + 1)
                    if g == 0 and not first:
                        act.wait_ge(sem["idx"], T)
                    A(qT[:, 4 * g:4 * g + 4, :], q_ps[g % 2][:], ACT.Copy).then_inc(sem["qT"], 1)
                if part >= 2:
                    g = part - 2
                    act.wait_ge(sem["s_ps"], 4 * T + g + 1)
                    A(s_buf[:, BANK * g:BANK * (g + 1)], s_ps[g % 2][:], ACT.Copy).then_inc(sem["s"], 1)

            def exponentials(T):
                act.wait_ge(sem["shifted"], T + 1)
                A(ex[:], ex[:], ACT.Exp).then_inc(sem["ex"], 1)

            def final_root(t):
                act.wait_ge(sem["summed"], 2 * t + 2)
                A(junk, row(t), ACT.Square, accum_out=stat[:, 4:5]).then_inc(sem["ssf"], 1)
                act.wait_ge(sem["ssf"], t + 1)
                A(stat[:, 5:6], stat[:, 4:5], ACT.Sqrt, bias=cst[:, C_EPS:C_EPS + 1], scale=1.0 / D).then_inc(sem["rmsf"], 1)

            def tile(t, first=False, last=False):
                for n in range(SLOTS):
                    h, k = divmod(n, TOPK)
                    if k == 0:
                        cols = slice(n, n + TOPK)
                        act.wait_ge(sem["u_free"], t * SLOTS + UR + n + TOPK)
                        A(acts[:, cols], dots[:, cols], ACT.Gelu).then_inc(sem["gelu"], 1)
                        if n == 0 and not last:
                            row_root(t + 1)
                        act.wait_ge(sem["coef"], t * PH + h + 1)
                    if n == 7 and not first:
                        final_root(t - 1)
                    if n - 2 in ROUTE_AT and not last:
                        route(t + 1, ROUTE_AT[n - 2])
                    if n == 76 and not last:
                        exponentials(t + 1)
                    act.wait_ge(sem["v_free"], t * SLOTS + n + 1)
                    A(diag[:, n % DR, :], ident, ACT.Copy, scale=coef[:, n:n + 1]).then_inc(sem["diag"], 1)

            def copy_mixed(t, first=False):
                for i in range(2):
                    act.wait_ge(sem["oT_ps"], 2 * t + i + 1)
                    if not first and i == 0:
                        act.wait_ge(sem["out_ps"], 2 * t)
                    A(xT[:, 4 * i:4 * i + 4, :], x_ps[i][:], ACT.Copy).then_inc(sem["oT"], 1)

            copy_mixed(0, first=True)
            with act.Fori(1, TILES) as t:
                copy_mixed(t)
            for g, bank in enumerate(q_ps + s_ps):
                act.wait_ge(sem["skT_ps"], g + 1)
                A(skT[:, 4 * g:4 * g + 4, :], bank[:], ACT.Copy).then_inc(sem["skT"], 1)
            act.wait_ge(sem["h"], 2 * TILES)
            row_root(0)
            for part in range(6):
                route(0, part, first=True)
            exponentials(0)
            tile(0, first=True)
            with act.Fori(1, TILES - 1) as t:
                tile(t)
            tile(TILES - 1, last=True)
            final_root(TILES - 1)

        @block.vector
        def _(dve):
            V = nc.vector

            def normed(T, first=False):
                dve.wait_ge(sem["rms2"], T + 1)
                V.reciprocal(stat[:, 2:3], stat[:, 1:2]).then_inc(sem["rstd2"], 1)
                dve.wait_ge(sem["rstd2"], T + 1)
                V.scalar_tensor_tensor(xn_next[:], row(T), stat[:, 2:3], gain2[:], ALU.mult, ALU.mult).then_inc(sem["xn2"], 1)

            def route(T):
                step = Steps(sem["route"], ROUTE_STEPS, T)
                sub = [s_buf[:, NK * n:NK * (n + 1)] for n in range(HC)]
                for g in range(4):
                    dve.wait_ge(sem["s"], 4 * T + g + 1)
                    dve.nop(nofuse=True)
                    four = range(4 * g, 4 * g + 4)
                    for half in range(2):
                        eight = slice(8 * half, 8 * half + 8)
                        for n in four:
                            last = V.max(top[:, n, eight], sub[n])
                        step.done(last)
                        yield
                        step.wait(dve)
                        for n in four:
                            last = V.max_index(topi[:, n, eight], top[:, n, eight], sub[n])
                        if half == 0:
                            step.done(last)
                            step.wait(dve)
                            for n in four:
                                last = V.match_replace(sub[n], top[:, n, eight], sub[n], LOWEST)
                        step.done(last)
                        yield
                        step.wait(dve)
                V.tensor_copy(topf[:], topi[:])
                t4 = top[:].rearrange("p (h c) k -> p h c k", c=SIDES)
                for hh in range(2):
                    hs = slice(4 * hh, 4 * hh + 4)
                    c4 = cand[:, 1024 * hh:1024 * (hh + 1)].rearrange("p (h a b) -> p h a b", a=TOPK, b=TOPK)
                    last = V.tensor_tensor(c4, t4[:, hs, 0, :].unsqueeze(3).to_broadcast([P, 4, TOPK, TOPK]),
                                           t4[:, hs, 1, :].unsqueeze(2).to_broadcast([P, 4, TOPK, TOPK]), ALU.add)
                    yield
                step.done(last)
                step.wait(dve)
                sums = [cand[:, 256 * h:256 * (h + 1)] for h in range(PH)]
                pos3 = pos[:].rearrange("p (h k) -> p h k", k=TOPK)
                for half in range(2):
                    eight = slice(8 * half, 8 * half + 8)
                    for h in range(PH):
                        last = V.max(best[:, h, eight], sums[h])
                        if h == 3:
                            yield
                    step.done(last)
                    yield
                    step.wait(dve)
                    for h in range(PH):
                        last = V.max_index(pos3[:, h, eight], best[:, h, eight], sums[h])
                        if h == 3:
                            yield
                    step.done(last)
                    yield
                    if half == 0:
                        step.wait(dve)
                        for h in range(PH):
                            last = V.match_replace(sums[h], best[:, h, eight], sums[h], LOWEST)
                            if h == 3:
                                yield
                        step.done(last)
                        yield
                        step.wait(dve)
                V.tensor_tensor(ex[:], best[:], best[:, :, 0:1].to_broadcast([P, PH, TOPK]), ALU.subtract)\
                 .then_inc(sem["shifted"], 1)
                step.wait(dve)
                V.tensor_scalar(pos2[:, 0, :], pos[:], 4, None, ALU.logical_shift_right)
                step.done(V.tensor_scalar(pos2[:, 1, :], pos[:], 15, None, ALU.bitwise_and))
                step.wait(dve)
                step.done(V.tensor_copy(posf[:], pos2[:]))
                step.wait(dve)
                yield
                iota = cst[:, C_IOTA:C_IOTA + TOPK].unsqueeze(1).to_broadcast([P, SLOTS, TOPK])
                f4 = topf[:].rearrange("p (h c) k -> p h c k", c=SIDES)
                hot = s_buf.rearrange("p (n a) -> p n a", a=TOPK)
                for c in range(SIDES):
                    step.done(V.tensor_tensor(hot, posf[:, c, :].unsqueeze(2).to_broadcast([P, SLOTS, TOPK]), iota, ALU.is_equal))
                    yield
                    step.wait(dve)
                    for h in range(PH):
                        hh = hot[:, TOPK * h:TOPK * (h + 1), :]
                        last = V.tensor_tensor(hh, hh, f4[:, h, c, :].unsqueeze(1).to_broadcast([P, TOPK, TOPK]), ALU.mult)
                    step.done(last)
                    yield
                    step.wait(dve)
                    step.done(V.tensor_reduce(key[:, c, :], hot, AX.X, ALU.add))
                    yield
                    step.wait(dve)
                assert step.n == ROUTE_STEPS, step.n

            def publish(T, first=False):
                if not first:
                    dve.wait_ge(sem["staged"], PH * T)
                dve.wait_ge(sem["route"], ROUTE_STEPS * (T + 1))
                V.scalar_tensor_tensor(idx_next[:], key[:, 0, :], float(NK), key[:, 1, :], ALU.mult, ALU.add)\
                 .then_inc(sem["idx"], 1)
                dve.wait_ge(sem["ex"], T + 1)
                V.tensor_reduce(soft[:, 0:8], ex[:], AX.X, ALU.add).then_inc(sem["soft"], 1)
                dve.wait_ge(sem["soft"], 2 * T + 1)
                V.reciprocal(soft[:, 8:16], soft[:, 0:8]).then_inc(sem["soft"], 1)
                dve.wait_ge(sem["soft"], 2 * T + 2)
                V.tensor_tensor(g_next[:].rearrange("p (h k) -> p h k", k=TOPK), ex[:],
                                soft[:, 8:16].unsqueeze(2).to_broadcast([P, PH, TOPK]), ALU.mult).then_inc(sem["g_next"], 1)

            def weigh(t, h):
                dve.wait_ge(sem["g_cur"], t + 1)
                cols = slice(TOPK * h, TOPK * (h + 1))
                dve.wait_ge(sem["gelu"], t * PH + h + 1)
                V.tensor_tensor(coef[:, cols], acts[:, cols], g_cur[:, cols], ALU.mult).then_inc(sem["coef"], 1)

            def add_residual(t):
                dve.wait_ge(sem["v_free"], (t + 1) * SLOTS + VR)
                for i in range(2):
                    hs = row(t)[:, BANK * i:BANK * (i + 1)]
                    V.tensor_tensor(hs, hs, o_ps[i][:], ALU.add).then_inc(sem["summed"], 1)

            def final_norm(t):
                dve.wait_ge(sem["rmsf"], t + 1)
                V.reciprocal(stat[:, 6:7], stat[:, 5:6]).then_inc(sem["rstdf"], 1)
                dve.wait_ge(sem["rstdf"], t + 1)
                V.scalar_tensor_tensor(row(t), row(t), stat[:, 6:7], gainf[:], ALU.mult, ALU.mult).then_inc(sem["y"], 1)

            def tile(t, first=False, last=False):
                dve.wait_ge(sem["g_next"], t + 1)
                if not first:
                    dve.wait_ge(sem["u_free"], UR + SLOTS * t)
                V.tensor_copy(xn_cur[:], xn_next[:]).then_inc(sem["cur"], 1)
                dve.wait_ge(sem["cur"], t + 1)
                routing = None if last else route(t + 1)
                for n in range(SLOTS):
                    h, k = divmod(n, TOPK)
                    dve.wait_ge(sem["u_in"][n % UR], 16 * (t * (SLOTS // UR) + n // UR + 1))
                    V.scalar_tensor_tensor(urow[:, n % UR, :], urow[:, n % UR, :], 1.0, xn_cur[:], ALU.mult, ALU.mult,
                                           accum_out=dots[:, n:n + 1]).then_inc(sem["u_free"], 1)
                    if k == 1 and h:
                        weigh(t, h - 1)
                    if n == 1:
                        if not first:
                            weigh(t - 1, PH - 1)
                            dve.wait_ge(sem["coef"], PH * t)
                        V.tensor_copy(g_cur[:], g_next[:]).then_inc(sem["g_cur"], 1)
                    if n == 19 and not first:
                        add_residual(t - 1)
                    if n == 20 and not last:
                        normed(t + 1)
                    if n == 27 and not first:
                        final_norm(t - 1)
                    if not last and (n >= 60 or n >= 36 and n % 2 == 0):
                        next(routing, None)
                    if not last and n == 119:
                        for _ in routing:
                            pass
                        publish(t + 1)
                if last:
                    weigh(t, PH - 1)

            dve.wait_ge(sem["x_again"], 16)
            with dve.Fori(0, TILES) as t:
                for i in range(2):
                    half = slice(BANK * i, BANK * (i + 1))
                    dve.wait_ge(sem["out_ps"], 2 * t + 1 + i)
                    V.tensor_tensor(row(t)[:, half], x_in[:, bass.ds(t, 1), half].rearrange("p o d -> p (o d)"),
                                    o_ps[i][:], ALU.add).then_inc(sem["h"], 1)
            V.memset(cred[:, 0:1], 0.0).then_inc(sem["u_free"], UR)
            V.memset(cred[:, 1:2], 0.0).then_inc(sem["v_free"], VR)
            dve.wait_ge(sem["gain2_in"], 32)
            normed(0)
            for _ in route(0):
                pass
            publish(0, first=True)
            tile(0, first=True)
            with dve.Fori(1, TILES - 1) as t:
                tile(t)
            tile(TILES - 1, last=True)
            add_residual(TILES - 1)
            final_norm(TILES - 1)


NAMES_MIX = """pad_zeroed x0_in gain1_in cst_in w_in_in x_in rope_in gate_in hg_in xn S_new xT_ps xT decay_last
 ga_ps gate_g gqk_ps gaT z_ps gate_r rqk_ps gqk gv_ps log_a R_new cum_ps rope rv_ps gv gg_ps gqkk norm_g gT_ps norm_r
 rT_ps rv rg_ps gqs gT att_ps rT rqx kv_g_ps kv_r_ps att S_mid state0 o_ps o 
 ss rms absz decay sq_g centred sq_r hss hroot rstd roped kz hmean hrstd scaled mixed""".split()
NAMES_PEER = """mixed_at w_out_in x_again oT_ps oT out_ps h sk_in gain2_in w_q_in y stored idx staged u_free v_free xn2 x2T_ps x2T qT q_ps s s_ps diag summed skT_ps
 skT ss2 rms2 shifted ex ssf rmsf gelu coef rstd2 route soft g_next rstdf cur g_cur""".split()


def build(nc, io, out):
    with ExitStack() as ctx:
        sem = {n: ctx.enter_context(nc.semaphore(n)) for n in NAMES_MIX + NAMES_PEER}
        sem["u_in"] = [ctx.enter_context(nc.semaphore(f"u_in{i}")) for i in range(UR)]
        sem["v_in"] = [ctx.enter_context(nc.semaphore(f"v_in{i}")) for i in range(VR)]
        shared = {
            "h": ctx.enter_context(nc.sbuf_tensor("h_all", [P, TILES + 1, D], F32)),
            "cst": ctx.enter_context(nc.sbuf_tensor("cst_sb", [P, C_END], F32)),
        }
        with nc.Block() as block:
            mixer_phase(nc, block, io, shared, sem)
        with nc.Block() as block:
            peer_phase(nc, block, io, out, shared, sem)


def constants():
    import numpy as np
    f = np.float32
    c, m = np.zeros((P, C_END), f), np.zeros((P, M_END), f)
    rope = np.zeros((P, TILES + 1, ROPE_W), f)
    j, i = np.arange(P)[:, None], np.arange(P)[None, :]
    same = (j // CH) == (i // CH)
    c[:, C_ID:C_ID + P] = np.eye(P)
    m[:, M_TRI:M_TRI + P] = (same & (j <= i)) / 16.0
    m[:, M_REV:M_REV + P] = (same & (j > i)) / 16.0
    m[:, M_MASK:M_MASK + P] = same & (j <= i)
    m[:, M_IND:M_IND + 2] = (j // CH == np.arange(2)[None, :]) / 16.0
    c[:, C_ONE] = 1.0
    c[:, C_EPS] = EPS
    c[:, C_IOTA:C_IOTA + TOPK] = np.arange(TOPK)
    lg = np.log1p(-(2.0 ** (-5.0 - np.arange(HEADS))))
    scale = DK ** -0.5
    for h in range(HEADS):
        m[:, M_DMAT + P * h:M_DMAT + P * (h + 1)] = np.where(j <= i, np.exp(lg[h] * np.maximum(i - j, 0)), 0.0) * scale
        m[:, M_ZETA + h] = np.exp(lg[h] * (P - 1 - np.arange(P))) * scale
        rows = slice(DK * (h % 2), DK * (h % 2) + DK)
        m[rows, M_XI + P * (h // 2):M_XI + P * (h // 2 + 1)] = np.exp(lg[h] * (np.arange(P) + 1.0))[None, :]
        m[rows, M_GAM + h // 2] = np.exp(lg[h] * P)
    inv_freq = (f(10000.0) ** (-np.arange(0, DK, 2, dtype=f) / f(DK))).astype(f)
    for t in range(TILES + 1):
        pos = (np.arange(P) + P * t - (P - NMETA)).astype(f)
        ang = (pos[:, None] * inv_freq[None, :]).astype(f).astype(np.float64)
        rope[:, t, 0:32] = np.cos(ang)
        rope[:, t, 32:64] = -np.sin(ang)
        rope[:, t, 64:96] = np.sin(ang)
    return c, m, rope


_INS = ["x", "meta_tokens", "norm1_gain", "w_in", "gla_gate_w2", "gla_gate_b", "gla_norm_gain", "ret_norm_gain",
        "ret_norm_bias", "w_out", "norm2_gain", "peer_w_q", "peer_subkeys", "peer_u", "peer_v", "final_gain"]


def kernel(**inputs):
    import numpy as _np
    import concourse.bacc as _bacc
    from concourse import mybir as _mybir
    from concourse.bass_utils import run_bass_kernel_spmd as _run

    nc = _bacc.Bacc("TRN2", target_bir_lowering=False, num_devices=1)
    arrays, io = {}, {}
    for name in _INS:
        arrays[f"in_{name}"] = _np.ascontiguousarray(inputs[name])
    arrays["in_cst"], arrays["in_mix"], arrays["in_rope"] = constants()
    for name, a in arrays.items():
        io[name[3:]] = nc.dram_tensor(name, a.shape, _mybir.dt.from_np(a.dtype), kind="ExternalInput").ap()
    out = nc.dram_tensor("out_dram", (1, SEQ, D), _mybir.dt.float32, kind="ExternalOutput").ap()
    build(nc, io, out)
    r = _run(nc, [arrays], core_ids=[0])
    return r.results[0]["out_dram"]
```

```python
import concourse.bass as bass
from concourse import mybir
from contextlib import ExitStack
from itertools import chain

F32 = mybir.dt.float32
U32 = mybir.dt.uint32
ALU = mybir.AluOpType
ACT = mybir.ActivationFunctionType
AX = mybir.AxisListType

P = 128
D = 1024
KC = D // P
HEADS = 4
DK, DV = 64, 128
PAIRS = HEADS // 2
CH = 64
SEQ, NMETA = 1024, 16
TILES = SEQ // P
BANK = 512
EPS = 1e-6
GQK, GV, GG, GA, RQK, RV, RG = 0, 512, 1024, 1536, 1552, 2064, 2576
RANK = 16
IN_WIDTH = 3088
W_PARTS = [(GA, RV), (GQK, GV), (GV, GG), (RV, RG), (GG, GA), (RG, IN_WIDTH)]
PH, NK, TOPK = 8, 128, 16
SIDES = 2
HC = PH * SIDES
SLOTS = PH * TOPK
UR, VR, DR, HR = 4, 4, 8, 4
LOWEST = -3.4028235e38
C_ID, C_ONE, C_EPS, C_IOTA, C_END = 0, 128, 129, 130, 146
M_TRI, M_REV, M_MASK, M_DMAT, M_XI, M_ZETA, M_GAM, M_IND, M_END = 0, 128, 256, 384, 896, 1152, 1156, 1158, 1160
ROPE_W = 96


def mixer_phase(nc, block, io, shared, sem):
    cst = shared["cst"]
    ident = cst[:, C_ID:C_ID + P]
    with ExitStack() as ctx:
        def sb(name, shape, dt=F32):
            return ctx.enter_context(nc.sbuf_tensor(name, shape, dt))

        def ps(name):
            return ctx.enter_context(nc.psum_tensor(name, [P, BANK], F32))

        h_all = sb("h_all", [P, TILES + 1, D])
        w_in = sb("w_in_sb", [P, KC, IN_WIDTH])
        mix = sb("mix_sb", [P, M_END])
        rope = sb("rope_sb", [P, TILES + 1, ROPE_W])
        gain1 = sb("gain1", [P, D])
        xn = sb("xn", [P, D])
        xT = sb("xT", [P, KC, P])
        junk = sb("junk", [P, D], mybir.dt.bfloat16)
        stat = sb("stat", [P, 4])
        gaT = sb("gaT", [RANK + 1, P])
        w2b = sb("w2b", [RANK + 1, HEADS * DK])
        absz = sb("absz", [P, 256])
        log_a = sb("log_a", [P, 256])
        decay = sb("decay", [P, 3, 256])
        a_last = sb("a_last", [P, PAIRS, 2])
        gqk = sb("gqk", [P, 512])
        gqkk = sb("gqkk", [P, 3, 256])
        gT = sb("gT", [P, PAIRS, P])
        gqs = sb("gqs", [P, PAIRS, 2, P])
        ropeA = sb("ropeA", [P, 512])
        rqk = sb("rqk", [P, 512])
        kz = sb("kz", [P, 256])
        rT = sb("rT", [P, 2 * PAIRS, P])
        rqx = sb("rqx", [P, PAIRS, P])
        att_g = sb("att_g", [P, HEADS, P])
        att_r = sb("att_r", [P, HEADS, P])
        v_g = sb("v_g", [P, 512])
        v_r = sb("v_r", [P, 512])
        gate = sb("gate", [P, D])
        S_prev = sb("S_prev", [P, PAIRS, 256])
        S_mid = sb("S_mid", [P, PAIRS, 256])
        R_prev = sb("R_prev", [P, PAIRS, 256])
        sq = sb("sq", [P, 512])
        sq2 = sb("sq2", [P, D])
        hstat = sb("hstat", [P, 32])
        hg = sb("hg", [P, 3, DV])

        o_sb = sb("o_sb", [P, 2, PAIRS, 2, DV])
        o_g = o_sb[:, 0].rearrange("p a e d -> p (a e d)")
        o_r = o_sb[:, 1].rearrange("p a e d -> p (a e d)")

        pa = [ps(f"pa{i}") for i in range(8)]
        pT = [pa[2], pa[3]]


        @block.sync
        def _(sp):
            sp.wait_ge(sem["pad_zeroed"], 1)
            sp.dma_start(h_all[P - NMETA:P, 0, :], io["meta_tokens"][:, :]).then_inc(sem["x0_in"], 16)
            sp.dma_start(cst[:], io["cst"][:, :]).then_inc(sem["cst_in"], 16)
            sp.dma_start(gain1[:], io["norm1_gain"][0:1, :].to_broadcast([P, D])).then_inc(sem["gain1_in"], 16)

            def columns(i):
                start, end = W_PARTS[i]
                sp.dma_start(w_in[:, :, start:end], io["w_in"][0].rearrange("(k p) n -> p k n", p=P)[:, :, start:end])\
                    .then_inc(sem["w_in_in"][i], 16)

            columns(0)
            columns(1)
            sp.dma_start(w2b[0:RANK, :], io["gla_gate_w2"][0]).then_inc(sem["gate_in"], 16)
            sp.dma_start(w2b[RANK:RANK + 1, :], io["gla_gate_b"][:, :]).then_inc(sem["gate_in"], 16)
            sp.dma_start(mix[:], io["mix"][:, :]).then_inc(sem["mix_in"], 16)
            sp.dma_start(rope[:], io["rope"][:, :, :]).then_inc(sem["rope_in"], 16)
            columns(2)
            sp.dma_start(h_all[:, 1, :], io["x"][0, 0:P, :]).then_inc(sem["x1_in"], 16)
            for i in range(3, len(W_PARTS)):
                columns(i)
            sp.dma_start(h_all[:, 2:TILES + 1, :],
                         io["x"][0].rearrange("(t p) d -> p t d", p=P)[:, 1:TILES, :]).then_inc(sem["x_in"], 16)
            with sp.Fori(1, TILES + 1) as t:
                sp.wait_ge(sem["mixed"], t + 1)
                sp.dma_start(shared["mixed"].rearrange("t p d -> p t d")[:, bass.ds(t - 1, 1), :],
                             h_all[:, bass.ds(t, 1), :]).then_inc(sem["mixed_out"], 16)
            sp.wait_ge(sem["mixed_out"], 16 * TILES)

        @block.gpsimd
        def _(pool):
            for i, n in enumerate(("gla_norm_gain", "ret_norm_gain", "ret_norm_bias")):
                pool.dma_start(hg[:, i, :], io[n][0:1, :].to_broadcast([P, DV])).then_inc(sem["hg_in"], 16)

        @block.tensor
        def _(pe):
            def landed(prev, part):
                if not prev:
                    pe.wait_ge(sem["w_in_in"][part], 16)

            def project(bank, w, src, col, width=BANK):
                for k in range(KC):
                    last = nc.tensor.matmul(bank[:, 0:width], src[:, k, :], w[:, k, col:col + width],
                                            start=(k == 0), stop=(k == KC - 1))
                return last

            def transpose_rows(t, prev=True):
                pe.wait_ge(sem["xn"], t + 1)
                if prev:
                    pe.wait_ge(sem["S_new"], t - 1)
                for k in range(KC):
                    last = nc.tensor.transpose(pT[k // 4][:, P * (k % 4):P * (k % 4 + 1)],
                                               xn[:, P * k:P * (k + 1)], ident)
                    if k % 4 == 3:
                        last.then_inc(sem["xT_ps"], 1)

            def tile(t, prev=True, final=False):
                if not prev:
                    pe.wait_ge(sem["w_in_in"][0], 16)
                    pe.wait_ge(sem["xT"], 2)
                if prev:
                    pe.wait_ge(sem["decay_last"], t)
                for k in range(KC):
                    last = nc.tensor.matmul(pa[4][0:RANK, 0:P], w_in[:, k, GA:GA + RANK], xT[:, k, :],
                                            start=(k == 0), stop=(k == KC - 1))
                last.then_inc(sem["ga_ps"], 1)
                if prev:
                    pe.wait_ge(sem["gate_g"], t)
                landed(prev, 1)
                project(pa[0], w_in, xT, GQK).then_inc(sem["gqk_ps"], 1)
                pe.wait_ge(sem["gaT"], t + 1)
                if not prev:
                    pe.wait_ge(sem["gate_in"], 32)
                nc.tensor.matmul(pa[4][:, P:P + 256], gaT[:, :], w2b[:, :], start=True, stop=True).then_inc(sem["z_ps"], 1)
                if prev:
                    pe.wait_ge(sem["gate_r"], t)
                project(pa[1], w_in, xT, RQK).then_inc(sem["rqk_ps"], 1)
                pe.wait_ge(sem["gqk"], t + 1)
                landed(prev, 2)
                project(pa[0], w_in, xT, GV).then_inc(sem["gv_ps"], 1)
                pe.wait_ge(sem["log_a"], t + 1)
                if not prev:
                    pe.wait_ge(sem["mix_in"], 16)
                if prev:
                    pe.wait_ge(sem["R_new"], t)
                nc.tensor.matmul(pa[5][:, 0:256], mix[:, M_TRI:M_TRI + P], log_a[:], start=True, stop=True)
                nc.tensor.matmul(pa[5][:, 256:512], mix[:, M_REV:M_REV + P], log_a[:], start=True, stop=True)
                for p in range(PAIRS):
                    last = nc.tensor.matmul(pa[4][:, 384 + 2 * p:386 + 2 * p], log_a[:, P * p:P * (p + 1)],
                                            mix[:, M_IND:M_IND + 2], start=True, stop=True)
                last.then_inc(sem["cum_ps"], 1)
                pe.wait_ge(sem["rope"], t + 1)
                landed(prev, 3)
                project(pa[1], w_in, xT, RV).then_inc(sem["rv_ps"], 1)
                pe.wait_ge(sem["gv"], t + 1)
                landed(prev, 4)
                project(pa[0], w_in, xT, GG).then_inc(sem["gg_ps"], 1)
                pe.wait_ge(sem["gqkk"], t + 1)
                if prev:
                    pe.wait_ge(sem["o"], 2 * t)
                for i in range(4):
                    last = nc.tensor.transpose(pa[6][:, P * i:P * (i + 1)],
                                               gqkk[:, i // 2, P * (i % 2):P * (i % 2 + 1)], ident)
                last.then_inc(sem["gT_ps"], 1)
                for i in range(4):
                    last = nc.tensor.transpose(pa[7][:, P * i:P * (i + 1)], rqk[:, P * i:P * (i + 1)], ident)
                last.then_inc(sem["rT_ps"], 1)
                pe.wait_ge(sem["rv"], t + 1)
                landed(prev, 5)
                project(pa[1], w_in, xT, RG).then_inc(sem["rg_ps"], 1)
                if not final:
                    transpose_rows(t + 1, prev)
                pe.wait_ge(sem["gqs"], t + 1)
                pe.wait_ge(sem["gT"], t + 1)
                pe.wait_ge(sem["rT"], t + 1)
                for h in range(HEADS):
                    rows = slice(DK * (h % 2), DK * (h % 2) + DK)
                    for c in range(2):
                        nc.tensor.matmul(pa[6 + h % 2][:, P * (h // 2) + CH * c:P * (h // 2) + CH * (c + 1)], gT[rows, h // 2, :],
                                         gqs[rows, h // 2, c, CH * c:CH * (c + 1)], start=True, stop=True)
                for h in range(HEADS):
                    rows = slice(DK * (h % 2), DK * (h % 2) + DK)
                    last = nc.tensor.matmul(pa[6 + h % 2][:, 256 + P * (h // 2):256 + P * (h // 2 + 1)], rT[rows, 2 + h // 2, :],
                                            rT[rows, h // 2, :], start=True, stop=True)
                    if h >= 2:
                        last.then_inc(sem["att_ps"], 1)
                if not final:
                    pe.wait_ge(sem["xT"], 2 * t + 4)
                for c in range(2):
                    for p in range(PAIRS):
                        rows = slice(CH * c, CH * (c + 1))
                        last = nc.tensor.matmul(pT[c][:, 256 * p:256 * (p + 1)], gqkk[rows, 2, P * p:P * (p + 1)],
                                                v_g[rows, 256 * p:256 * (p + 1)], start=True, stop=True)
                    last.then_inc(sem["kv_g_ps"], 1)
                for p in range(PAIRS):
                    last = nc.tensor.matmul(pa[5][:, 256 * p:256 * (p + 1)], kz[:, P * p:P * (p + 1)],
                                            v_r[:, 256 * p:256 * (p + 1)], start=True, stop=True)
                last.then_inc(sem["kv_r_ps"], 1)
                pe.wait_ge(sem["att"], t + 1)
                pe.wait_ge(sem["rqx"], t + 1)
                pe.wait_ge(sem["S_mid"], t + 1)
                if not prev:
                    pe.wait_ge(sem["state0"], 1)
                for h in range(HEADS):
                    rows = slice(DK * (h % 2), DK * (h % 2) + DK)
                    vc = slice(P * (h % 2), P * (h % 2) + P)
                    o = pa[6 + h % 2][:, P * (h // 2):P * (h // 2 + 1)]
                    nc.tensor.matmul(o, att_g[:, h, :], v_g[:, P * h:P * (h + 1)], start=True, stop=False)
                    nc.tensor.matmul(o, gqs[rows, h // 2, 0, :], S_prev[rows, h // 2, vc], start=False, stop=False)
                    nc.tensor.matmul(o, gqs[rows, h // 2, 1, :], S_mid[rows, h // 2, vc], start=False, stop=True)
                for h in range(HEADS):
                    rows = slice(DK * (h % 2), DK * (h % 2) + DK)
                    vc = slice(P * (h % 2), P * (h % 2) + P)
                    o = pa[6 + h % 2][:, 256 + P * (h // 2):256 + P * (h // 2 + 1)]
                    nc.tensor.matmul(o, att_r[:, h, :], v_r[:, P * h:P * (h + 1)], start=True, stop=False)
                    last = nc.tensor.matmul(o, rqx[rows, h // 2, :], R_prev[rows, h // 2, vc], start=False, stop=True)
                    if h >= 2:
                        last.then_inc(sem["o_ps"], 1)

            pe.wait_ge(sem["cst_in"], 16)
            transpose_rows(0, prev=False)
            tile(0, prev=False)
            with pe.Fori(1, TILES) as t:
                tile(t)
            tile(TILES, final=True)

        @block.scalar
        def _(act):
            A = nc.scalar.activation

            def row_root(t):
                A(junk[:], h_all[:, bass.ds(t, 1), :], ACT.Square, accum_out=stat[:, 0:1]).then_inc(sem["ss"], 1)
                act.wait_ge(sem["ss"], t + 1)
                A(stat[:, 1:2], stat[:, 0:1], ACT.Sqrt, bias=cst[:, C_EPS:C_EPS + 1], scale=1.0 / D).then_inc(sem["rms"], 1)

            def copy_rows(t):
                for i in range(2):
                    act.wait_ge(sem["xT_ps"], 2 * t + i + 1)
                    A(xT[:, 4 * i:4 * i + 4, :], pT[i][:], ACT.Copy).then_inc(sem["xT"], 1)

            def tile(t, prev=True, final=False):
                if not final:
                    row_root(t + 1)
                act.wait_ge(sem["ga_ps"], t + 1)
                A(gaT[0:RANK, :], pa[4][0:RANK, 0:P], ACT.Copy).then_inc(sem["gaT"], 1)
                act.wait_ge(sem["gqk_ps"], t + 1)
                A(gqk[:], pa[0][:], ACT.Copy).then_inc(sem["gqk"], 1)
                act.wait_ge(sem["z_ps"], t + 1)
                A(absz[:], pa[4][:, P:P + 256], ACT.Abs).then_inc(sem["absz"], 1)
                act.wait_ge(sem["absz"], 3 * t + 1)
                A(absz[:], absz[:], ACT.Exp, scale=-1.0).then_inc(sem["absz"], 1)
                act.wait_ge(sem["absz"], 3 * t + 2)
                A(absz[:], absz[:], ACT.Ln, bias=cst[:, C_ONE:C_ONE + 1]).then_inc(sem["absz"], 1)
                act.wait_ge(sem["gv_ps"], t + 1)
                A(v_g[:], pa[0][:], ACT.Copy).then_inc(sem["gv"], 1)
                act.wait_ge(sem["cum_ps"], t + 1)
                A(a_last[:], pa[4][:, 384:388], ACT.Exp).then_inc(sem["decay_last"], 1)
                A(decay[:, 0, :], pa[5][:, 0:256], ACT.Exp)
                A(decay[:, 1, :], pa[5][:, 0:256], ACT.Exp, scale=-1.0)
                A(decay[:, 2, :], pa[5][:, 256:512], ACT.Exp).then_inc(sem["decay"], 1)
                act.wait_ge(sem["rv_ps"], t + 1)
                A(v_r[:], pa[1][:], ACT.Copy).then_inc(sem["rv"], 1)
                act.wait_ge(sem["gg_ps"], t + 1)
                A(gate[:, 0:512], pa[0][:], ACT.Silu).then_inc(sem["gate_g"], 1)
                act.wait_ge(sem["gqs"], t + 1)
                A(gT[:], pa[6][:, 256:512], ACT.Copy).then_inc(sem["gT"], 1)
                act.wait_ge(sem["rT_ps"], t + 1)
                A(rT[:], pa[7][:], ACT.Copy).then_inc(sem["rT"], 1)
                act.wait_ge(sem["rg_ps"], t + 1)
                A(gate[:, 512:1024], pa[1][:], ACT.Silu).then_inc(sem["gate_r"], 1)
                if not final:
                    copy_rows(t + 1)
                for e in range(2):
                    act.wait_ge(sem["o_ps"], 2 * t + e + 1)
                    A(o_sb[:, :, :, e, :], pa[6 + e][:].rearrange("p (g a d) -> p g a d", g=2, a=PAIRS), ACT.Copy).then_inc(sem["o"], 1)
                act.wait_ge(sem["o"], 2 * t + 2)
                A(sq[:], o_g, ACT.Square).then_inc(sem["sq_g"], 1)
                act.wait_ge(sem["centred"], t + 1)
                A(sq2[:, 512:1024], sq2[:, 0:512], ACT.Square).then_inc(sem["sq_r"], 1)
                act.wait_ge(sem["hss"], t + 1)
                A(hstat[:, 8:16], hstat[:, 0:8], ACT.Sqrt, bias=cst[:, C_EPS:C_EPS + 1], scale=1.0 / DV).then_inc(sem["hroot"], 1)

            act.wait_ge(sem["cst_in"], 16)
            act.wait_ge(sem["x0_in"], 16)
            row_root(0)
            copy_rows(0)
            act.wait_ge(sem["x1_in"], 16)
            tile(0, prev=False)
            act.wait_ge(sem["x_in"], 16)
            with act.Fori(1, TILES) as t:
                tile(t)
            tile(TILES, final=True)

        @block.vector
        def _(dve):
            V = nc.vector

            def heads(ap, n=DV):
                return ap.rearrange("p (h d) -> p h d", d=n)

            def normed(t, prev=True):
                dve.wait_ge(sem["rms"], t + 1)
                V.reciprocal(stat[:, 2:3], stat[:, 1:2]).then_inc(sem["rstd"], 1)
                dve.wait_ge(sem["rstd"], t + 1)
                if prev:
                    dve.wait_ge(sem["xT_ps"], 2 * t)
                V.scalar_tensor_tensor(xn[:], h_all[:, bass.ds(t, 1), :].rearrange("p o d -> p (o d)"), stat[:, 2:3],
                                       gain1[:], ALU.mult, ALU.mult).then_inc(sem["xn"], 1)

            def tile(t, prev=True, final=False):
                dve.wait_ge(sem["absz"], 3 * t + 3)
                if prev:
                    dve.wait_ge(sem["cum_ps"], t)
                V.scalar_tensor_tensor(log_a[:], pa[4][:, P:P + 256], 0.0, absz[:], ALU.min, ALU.subtract).then_inc(sem["log_a"], 1)
                dve.wait_ge(sem["rqk_ps"], t + 1)
                src = pa[1][:].rearrange("p (n s c) -> p n s c", s=2, c=DK // 2)
                tmp = ropeA[:].rearrange("p (n s c) -> p n s c", s=2, c=DK // 2)
                dst = rqk[:].rearrange("p (n s c) -> p n s c", s=2, c=DK // 2)
                rt = rope[:, bass.ds(t, 1), :]
                cos = rt[:, :, 0:32].to_broadcast([P, 8, 32])
                for s in range(2):
                    V.tensor_tensor(dst[:, :, s, :], src[:, :, s, :], cos, ALU.mult)
                for s in range(2):
                    sin = rt[:, :, 32 + 32 * s:64 + 32 * s].to_broadcast([P, 8, 32])
                    last = V.tensor_tensor(tmp[:, :, s, :], src[:, :, 1 - s, :], sin, ALU.mult)
                last.then_inc(sem["rope"], 1)
                dve.wait_ge(sem["rope"], t + 1)
                V.tensor_tensor(rqk[:], rqk[:], ropeA[:], ALU.add).then_inc(sem["roped"], 1)
                dve.wait_ge(sem["roped"], t + 1)
                zeta = mix[:, M_ZETA:M_ZETA + HEADS].unsqueeze(2).to_broadcast([P, HEADS, DK])
                V.tensor_tensor(heads(kz[:], DK), heads(rqk[:, 256:512], DK), zeta, ALU.mult).then_inc(sem["kz"], 1)
                dve.wait_ge(sem["decay"], t + 1)
                dve.wait_ge(sem["gqk"], t + 1)
                V.scalar_tensor_tensor(gqkk[:, 0, :], gqk[:, 0:256], DK ** -0.5, decay[:, 0, :], ALU.mult, ALU.mult)
                V.tensor_tensor(gqkk[:, 1, :], gqk[:, 256:512], decay[:, 1, :], ALU.mult)
                V.tensor_tensor(gqkk[:, 2, :], gqk[:, 256:512], decay[:, 2, :], ALU.mult).then_inc(sem["gqkk"], 1)
                if not final:
                    normed(t + 1)
                dve.wait_ge(sem["gT_ps"], t + 1)
                for c in range(2):
                    cs = slice(CH * c, CH * (c + 1))
                    last = V.tensor_copy(gqs[:, :, c, cs], pa[6][:, 0:256].rearrange("p (a i) -> p a i", i=P)[:, :, cs])
                last.then_inc(sem["gqs"], 1)
                dve.wait_ge(sem["rT"], t + 1)
                V.tensor_tensor(rqx[:], rT[:, 0:PAIRS, :],
                                mix[:, M_XI:M_XI + 256].rearrange("p (a i) -> p a i", i=P), ALU.mult).then_inc(sem["rqx"], 1)
                mask = mix[:, M_MASK:M_MASK + P].bitcast(U32).unsqueeze(1).to_broadcast([P, PAIRS, P])
                dmat = mix[:, M_DMAT:M_DMAT + 512].rearrange("p (a e i) -> p a e i", e=2, i=P)
                for e in range(2):
                    dve.wait_ge(sem["att_ps"], 2 * t + e + 1)
                    dve.nop(nofuse=True)
                    scores = pa[6 + e][:].rearrange("p (n i) -> p n i", i=P)
                    V.copy_predicated(att_g[:].rearrange("p (a e) i -> p a e i", e=2)[:, :, e, :], mask, scores[:, 0:2, :])
                    last = V.tensor_tensor(att_r[:].rearrange("p (a e) i -> p a e i", e=2)[:, :, e, :], scores[:, 2:4, :],
                                           dmat[:, :, e, :], ALU.mult)
                last.then_inc(sem["att"], 1)
                dve.wait_ge(sem["kv_g_ps"], 2 * t + 1)
                dve.wait_ge(sem["decay_last"], t + 1)
                for p in range(PAIRS):
                    last = V.scalar_tensor_tensor(S_mid[:, p, :], S_prev[:, p, :], a_last[:, p, 0:1],
                                                  pT[0][:, 256 * p:256 * (p + 1)], ALU.mult, ALU.add)
                last.then_inc(sem["S_mid"], 1)
                dve.wait_ge(sem["o_ps"], 2 * t + 2)
                dve.wait_ge(sem["kv_g_ps"], 2 * t + 2)
                dve.wait_ge(sem["S_mid"], t + 1)
                for p in range(PAIRS):
                    last = V.scalar_tensor_tensor(S_prev[:, p, :], S_mid[:, p, :], a_last[:, p, 1:2],
                                                  pT[1][:, 256 * p:256 * (p + 1)], ALU.mult, ALU.add)
                last.then_inc(sem["S_new"], 1)
                dve.wait_ge(sem["kv_r_ps"], t + 1)
                for p in range(PAIRS):
                    last = V.scalar_tensor_tensor(R_prev[:, p, :], R_prev[:, p, :], mix[:, M_GAM + p:M_GAM + p + 1],
                                                  pa[5][:, 256 * p:256 * (p + 1)], ALU.mult, ALU.add)
                last.then_inc(sem["R_new"], 1)
                dve.wait_ge(sem["o"], 2 * t + 2)
                V.tensor_reduce(hstat[:, 24:28], heads(o_r), AX.X, ALU.add).then_inc(sem["hmean"], 1)
                dve.wait_ge(sem["hmean"], 2 * t + 1)
                V.tensor_scalar(hstat[:, 28:32], hstat[:, 24:28], 1.0 / DV, None, ALU.mult).then_inc(sem["hmean"], 1)
                dve.wait_ge(sem["hmean"], 2 * t + 2)
                V.tensor_tensor(heads(sq2[:, 0:512]), heads(o_r),
                                hstat[:, 28:32].unsqueeze(2).to_broadcast([P, HEADS, DV]), ALU.subtract).then_inc(sem["centred"], 1)
                dve.wait_ge(sem["sq_g"], t + 1)
                V.tensor_reduce(hstat[:, 0:4], heads(sq[:]), AX.X, ALU.add)
                dve.wait_ge(sem["sq_r"], t + 1)
                V.tensor_reduce(hstat[:, 4:8], heads(sq2[:, 512:1024]), AX.X, ALU.add).then_inc(sem["hss"], 1)
                dve.wait_ge(sem["hroot"], t + 1)
                V.reciprocal(hstat[:, 16:24], hstat[:, 8:16]).then_inc(sem["hrstd"], 1)
                dve.wait_ge(sem["hrstd"], t + 1)
                mixed = h_all[:, bass.ds(t, 1), :].rearrange("p o d -> p (o d)")
                rs = hstat[:, 16:24].unsqueeze(2)
                V.tensor_tensor(heads(mixed[:, 0:512]), heads(o_g), rs[:, 0:4, :].to_broadcast([P, HEADS, DV]), ALU.mult)\
                 .then_inc(sem["norm_g"], 1)
                V.tensor_tensor(heads(mixed[:, 512:1024]), heads(sq2[:, 0:512]), rs[:, 4:8, :].to_broadcast([P, HEADS, DV]), ALU.mult)\
                 .then_inc(sem["norm_r"], 1)
                dve.wait_ge(sem["norm_r"], t + 1)
                V.tensor_tensor(heads(mixed[:, 0:512]), heads(mixed[:, 0:512]), hg[:, 0:1, :].to_broadcast([P, HEADS, DV]), ALU.mult)
                V.tensor_tensor(heads(mixed[:, 512:1024]), heads(mixed[:, 512:1024]), hg[:, 1:2, :].to_broadcast([P, HEADS, DV]), ALU.mult)\
                 .then_inc(sem["scaled"], 1)
                dve.wait_ge(sem["scaled"], 2 * t + 1)
                V.tensor_tensor(heads(mixed[:, 512:1024]), heads(mixed[:, 512:1024]), hg[:, 2:3, :].to_broadcast([P, HEADS, DV]), ALU.add)\
                 .then_inc(sem["scaled"], 1)
                dve.wait_ge(sem["scaled"], 2 * t + 2)
                dve.wait_ge(sem["gate_r"], t + 1)
                V.tensor_tensor(mixed, mixed, gate[:], ALU.mult).then_inc(sem["mixed"], 1)

            V.memset(h_all[:, 0, :], 0.0).then_inc(sem["pad_zeroed"], 1)
            V.memset(gaT[:], 1.0)
            V.memset(gqs[:], 0.0)
            V.memset(att_g[:], 0.0)
            V.memset(S_prev[:], 0.0)
            V.memset(R_prev[:], 0.0).then_inc(sem["state0"], 1)
            dve.wait_ge(sem["gain1_in"], 16)
            dve.wait_ge(sem["cst_in"], 16)
            dve.wait_ge(sem["state0"], 1)
            normed(0, prev=False)
            dve.wait_ge(sem["hg_in"], 48)
            dve.wait_ge(sem["mix_in"], 16)
            dve.wait_ge(sem["rope_in"], 16)
            tile(0, prev=False)
            with dve.Fori(1, TILES) as t:
                tile(t)
            tile(TILES, final=True)


class Steps:

    def __init__(self, sem, per_tile, tile):
        self.sem, self.per_tile, self.base, self.n = sem, per_tile, tile * per_tile, 0

    def done(self, instruction):
        self.n += 1
        instruction.then_inc(self.sem, 1)

    def wait(self, engine):
        engine.wait_ge(self.sem, self.base + self.n)
        engine.nop(nofuse=True)


MIX_AT = 4
OUT_AT = {n: i for i, n in enumerate((6, 7, 8, 9, 11, 12, 13, 14))}
ROWS_AT = 23
QUERY_AT = {26 + 2 * n: n for n in range(HC)}
SCORE_AT = {35 + 8 * g: g for g in range(4)}
SEARCH_AT = range(55, 119)
EXP_AT = 93
FIRST_EXP_AT = {0: 1, 12: 2, 28: 3}
FIRST_SEARCH_AT = range(3, 52)
PARTS = 4
PW = SLOTS // PARTS
HP = PH // PARTS
ROUTE_STEPS = 20 // PARTS + 14


def peer_phase(nc, block, io, out, shared, sem):
    cst = shared["cst"]
    ident = cst[:, C_ID:C_ID + P]
    with ExitStack() as ctx:
        def sb(name, shape, dt=F32):
            return ctx.enter_context(nc.sbuf_tensor(name, shape, dt))

        def ps(name):
            return ctx.enter_context(nc.psum_tensor(name, [P, BANK], F32))

        w_q = sb("w_q", [P, KC, HC * P])
        skT = sb("skT", [P, HC, NK])
        w_out = sb("w_out", [P, KC, D])
        h_ring = sb("h_ring", [P, HR, D])
        urow = sb("urow", [P, UR, D])
        s_buf = sb("s_buf", [P, HC * NK])
        cand = sb("cand", [P, PH * TOPK * TOPK])
        vrow = sb("vrow", [P, VR, D])
        diag = sb("diag", [P, DR, P])
        gain2 = sb("gain2", [P, D])
        gainf = sb("gainf", [P, D])
        xn_next = sb("xn_next", [P, D])
        xn_cur = sb("xn_cur", [P, D])
        xT = sb("xT_b", [P, KC, P])
        top = sb("top", [P, HC, TOPK])
        topi = sb("topi", [P, HC, TOPK], U32)
        topf = sb("topf", [P, HC, TOPK])
        best = sb("best", [P, PH, TOPK])
        pos = sb("pos", [P, SLOTS], U32)
        idx_next = sb("idx_next", [P, SLOTS], U32)
        idx_cur = sb("idx_cur", [P, SLOTS], U32)
        ex = sb("ex", [P, PH, TOPK])
        soft = sb("soft", [P, 16])
        g_next = sb("g_next", [P, SLOTS])
        g_cur = sb("g_cur", [P, SLOTS])
        dots = sb("dots", [P, SLOTS])
        acts = sb("acts", [P, SLOTS])
        coef = sb("coef", [P, SLOTS])
        junk = sb("junk_b", [P, D], mybir.dt.bfloat16)
        cred = sb("cred", [P, 2])
        stat = sb("stat_b", [P, 8])

        qT = cand[:].rearrange("p (n i) -> p n i", i=P)

        def part_of_cand(part, i):
            start = HC * P // PARTS * part + SIDES * PW * i
            return cand[:, start:start + SIDES * PW]

        sk_raw = [urow[:, 0, :], urow[:, 1, :]]
        o_ps = [ps("o_ps0"), ps("o_ps1")]
        x_ps = [ps("x_ps0"), ps("x_ps1")]
        q_ps = [ps("q_ps0"), ps("q_ps1")]
        s_ps = [ps("s_ps0"), ps("s_ps1")]

        def row(t):
            return h_ring[:, bass.ds(t % HR, 1), :].rearrange("p o d -> p (o d)")

        @block.sync
        def _(sp):
            def load_mixed(t):
                sp.dma_start(xn_next[:], shared["mixed"][t]).then_inc(sem["mixed_in"], 16)

            def load_x(t):
                sp.dma_start(h_ring[:, t % HR, :], io["x"][0, P * t:P * (t + 1), :]).then_inc(sem["x_again"], 16)

            load_mixed(0)
            sp.dma_start(urow[:].rearrange("p r (n d) -> p (r n) d", d=P)[:, 0:HC, :],
                         io["peer_subkeys"][0].rearrange("h c n d -> n (h c) d")).then_inc(sem["sk_in"], 16)
            for i in range(4):
                sp.dma_start(w_out[:, 2 * i:2 * i + 2, :], io["w_out"][0].rearrange("(k p) n -> p k n", p=P)[:, 2 * i:2 * i + 2, :])\
                    .then_inc(sem["w_out_in"][i], 16)
            load_x(0)
            sp.dma_start(gain2[:], io["norm2_gain"][0:1, :].to_broadcast([P, D])).then_inc(sem["gain2_in"], 16)
            for g in range(4):
                cols = slice(BANK * g, BANK * (g + 1))
                sp.dma_start(w_q[:, :, cols], io["peer_w_q"][0].rearrange("(k p) n -> p k n", p=P)[:, :, cols])\
                    .then_inc(sem["w_q_in"][g], 16)
            sp.dma_start(gainf[:], io["final_gain"].rearrange("(a d) -> a d", a=1).to_broadcast([P, D])).then_inc(sem["gainf_in"], 16)
            for t in range(TILES):
                if t + 1 < TILES:
                    sp.wait_ge(sem["cur"], t + 1)
                    if t + 1 >= HR:
                        sp.wait_ge(sem["stored"], 16 * (t + 2 - HR))
                    load_mixed(t + 1)
                    load_x(t + 1)
                if t:
                    sp.wait_ge(sem["y"], t)
                    sp.dma_start(out[0, P * (t - 1):P * t, :], h_ring[:, (t - 1) % HR, :]).then_inc(sem["stored"], 16)
            sp.wait_ge(sem["y"], TILES)
            sp.dma_start(out[0, P * (TILES - 1):P * TILES, :], h_ring[:, (TILES - 1) % HR, :]).then_inc(sem["stored"], 16)
            sp.wait_ge(sem["stored"], 16 * TILES)

        @block.gpsimd
        def _(pool):
            def gather(table, ring, n, size, free, landed, t):
                pool.wait_ge(free, t * SLOTS + n + 1)
                pool.nop(nofuse=True)
                pool.indirect_dma_start(out=ring[:, n % size, :], out_offset=None, in_=table,
                                        in_offset=bass.IndirectOffsetOnAxis(ap=idx_cur[:, n:n + 1], axis=0))\
                    .then_inc(landed[n % size], 16)

            def stage(t, h, count):
                cols = slice(TOPK * h, TOPK * (h + 1))
                pool.tensor_copy(idx_cur[:, cols], idx_next[:, cols]).then_inc(sem["staged"], 1)
                pool.wait_ge(sem["staged"], count + 1)

            def gather_u(t, n):
                gather(io["peer_u"][0], urow, n, UR, sem["u_free"], sem["u_in"], t)

            def tile(t, last=False):
                for h in range(PH):
                    ahead = (t, h + 1) if h < PH - 1 else (t + 1, 0)
                    if h == PH - 1 and not last:
                        pool.wait_ge(sem["idx"], PARTS * (t + 2))
                        pool.nop(nofuse=True)
                    if h < PH - 1 and (h + 1) % HP == 0:
                        pool.wait_ge(sem["idx"], PARTS * t + (h + 1) // HP + 1)
                        pool.nop(nofuse=True)
                    if not (h == PH - 1 and last):
                        stage(*ahead, PH * t + h + 1)
                    for k in range(TOPK):
                        if not (h == PH - 1 and last):
                            gather_u(ahead[0], TOPK * ahead[1] + k)
                        gather(io["peer_v"][0], vrow, TOPK * h + k, VR, sem["v_free"], sem["v_in"], t)

            pool.wait_ge(sem["idx"], 1)
            stage(0, 0, 0)
            for k in range(TOPK):
                gather_u(0, k)
            with pool.Fori(0, TILES - 1) as t:
                tile(t)
            tile(TILES - 1, last=True)

        @block.tensor
        def _(pe):
            def transpose_mixed(T):
                pe.wait_ge(sem["mixed_in"], 16 * (T + 1))
                for k in range(KC):
                    last = nc.tensor.transpose(x_ps[k // 4][:, P * (k % 4):P * (k % 4 + 1)],
                                               xn_next[:, P * k:P * (k + 1)], ident)
                    if k % 4 == 3:
                        last.then_inc(sem["oT_ps"], 1)

            def project_out(T, part):
                half, quarter = divmod(part, 4)
                if part == 0:
                    pe.wait_ge(sem["oT"], 2 * T + 2)
                for k in (2 * quarter, 2 * quarter + 1):
                    last = nc.tensor.matmul(q_ps[half][:], xT[:, k, :], w_out[:, k, BANK * half:BANK * (half + 1)],
                                            start=(k == 0), stop=(k == KC - 1))
                if quarter == 3:
                    last.then_inc(sem["out_ps"], 1)

            def transpose_rows(T):
                pe.wait_ge(sem["xn2"], T + 1)
                for k in range(KC):
                    last = nc.tensor.transpose(x_ps[k // 4][:, P * (k % 4):P * (k % 4 + 1)],
                                               xn_next[:, P * k:P * (k + 1)], ident)
                    if k % 4 == 3:
                        last.then_inc(sem["x2T_ps"], 1)

            def query(T, n):
                g = n // 4
                if n == 0:
                    pe.wait_ge(sem["x2T"], 2 * T + 2)
                if n % 4 == 0 and g >= 2:
                    pe.wait_ge(sem["qT"], 4 * T + g - 1)
                for k in range(KC):
                    last = nc.tensor.matmul(q_ps[g % 2][:, P * (n % 4):P * (n % 4 + 1)],
                                            w_q[:, k, P * n:P * (n + 1)], xT[:, k, :],
                                            start=(k == 0), stop=(k == KC - 1))
                if n % 4 == 3:
                    last.then_inc(sem["q_ps"], 1)

            def scores(T, g):
                pe.wait_ge(sem["qT"], 4 * T + g + 1)
                if g >= 2:
                    pe.wait_ge(sem["s"], 4 * T + g - 1)
                for n in range(4 * g, 4 * g + 4):
                    last = nc.tensor.matmul(s_ps[g % 2][:, P * (n % 4):P * (n % 4 + 1)],
                                            qT[:, n, :], skT[:, n, :], start=True, stop=True)
                last.then_inc(sem["s_ps"], 1)

            def ahead(T, n):
                if n == MIX_AT:
                    transpose_mixed(T)
                if n in OUT_AT:
                    project_out(T, OUT_AT[n])
                if n == ROWS_AT:
                    transpose_rows(T)
                if n in QUERY_AT:
                    query(T, QUERY_AT[n])
                if n in SCORE_AT:
                    scores(T, SCORE_AT[n])

            def tile(t, first=False, last=False):
                if not first:
                    pe.wait_ge(sem["summed"], 2 * t)
                for n in range(SLOTS):
                    if not last:
                        ahead(t + 1, n)
                    pe.wait_ge(sem["v_in"][n % VR], 16 * (t * (SLOTS // VR) + n // VR + 1))
                    pe.wait_ge(sem["diag"], t * SLOTS + n + 1)
                    for i in range(2):
                        product = nc.tensor.matmul(o_ps[i][:], diag[:, n % DR, :], vrow[:, n % VR, BANK * i:BANK * (i + 1)],
                                                   start=(n == 0), stop=(n == SLOTS - 1))
                    product.then_inc(sem["v_free"], 1)

            transpose_mixed(0)
            pe.wait_ge(sem["sk_in"], 16)
            for g, bank in enumerate(o_ps + s_ps):
                for n in range(4):
                    last = nc.tensor.transpose(bank[:, P * n:P * (n + 1)],
                                               sk_raw[g // 2][:, P * (4 * (g % 2) + n):P * (4 * (g % 2) + n + 1)], ident)
                last.then_inc(sem["skT_ps"], 1)
            for quarter in range(4):
                pe.wait_ge(sem["w_out_in"][quarter], 16)
                project_out(0, quarter)
                project_out(0, 4 + quarter)
            transpose_rows(0)
            pe.wait_ge(sem["skT"], 4)
            for g in range(4):
                pe.wait_ge(sem["w_q_in"][g], 16)
                for n in range(4 * g, 4 * g + 4):
                    query(0, n)
                scores(0, g)
            tile(0, first=True)
            with pe.Fori(1, TILES - 1) as t:
                tile(t)
            tile(TILES - 1, last=True)

        @block.scalar
        def _(act):
            A = nc.scalar.activation

            def row_root(T):
                act.wait_ge(sem["h"], 2 * T + 2)
                A(xT[:].rearrange("p k i -> p (k i)"), row(T), ACT.Square, accum_out=stat[:, 0:1]).then_inc(sem["ss2"], 1)
                act.wait_ge(sem["ss2"], T + 1)
                A(stat[:, 1:2], stat[:, 0:1], ACT.Sqrt, bias=cst[:, C_EPS:C_EPS + 1], scale=1.0 / D).then_inc(sem["rms2"], 1)

            def copy_mixed(T):
                for i in range(2):
                    act.wait_ge(sem["oT_ps"], 2 * T + i + 1)
                    A(xT[:, 4 * i:4 * i + 4, :], x_ps[i][:], ACT.Copy).then_inc(sem["oT"], 1)

            def copy_rows(T):
                for i in range(2):
                    act.wait_ge(sem["x2T_ps"], 2 * T + i + 1)
                    A(xT[:, 4 * i:4 * i + 4, :], x_ps[i][:], ACT.Copy).then_inc(sem["x2T"], 1)

            def copy_queries(T, g, first=False):
                act.wait_ge(sem["q_ps"], 4 * T + g + 1)
                if g == 0 and not first:
                    act.wait_ge(sem["idx"], PARTS * T)
                A(qT[:, 4 * g:4 * g + 4, :], q_ps[g % 2][:], ACT.Copy).then_inc(sem["qT"], 1)

            def copy_scores(T, g):
                act.wait_ge(sem["s_ps"], 4 * T + g + 1)
                A(s_buf[:, BANK * g:BANK * (g + 1)], s_ps[g % 2][:], ACT.Copy).then_inc(sem["s"], 1)

            def ahead(T, n):
                if n == MIX_AT:
                    copy_mixed(T)
                if n == ROWS_AT - 4:
                    row_root(T)
                if n == ROWS_AT:
                    copy_rows(T)
                if n in QUERY_AT and QUERY_AT[n] % 4 == 3:
                    copy_queries(T, QUERY_AT[n] // 4)
                if n in SCORE_AT:
                    copy_scores(T, SCORE_AT[n])
                if n == EXP_AT:
                    exponentials(T)

            def exponentials(T, parts=range(PARTS)):
                heads = slice(HP * parts[0], HP * (parts[-1] + 1))
                act.wait_ge(sem["shifted"], PARTS * T + parts[-1] + 1)
                A(ex[:, heads, :], ex[:, heads, :], ACT.Exp).then_inc(sem["ex"], len(parts))

            def final_root(t):
                act.wait_ge(sem["summed"], 2 * t + 2)
                A(junk[:], row(t), ACT.Square, accum_out=stat[:, 4:5]).then_inc(sem["ssf"], 1)
                act.wait_ge(sem["ssf"], t + 1)
                A(stat[:, 5:6], stat[:, 4:5], ACT.Sqrt, bias=cst[:, C_EPS:C_EPS + 1], scale=1.0 / D).then_inc(sem["rmsf"], 1)

            def tile(t, first=False, last=False):
                for n in range(SLOTS):
                    h, k = divmod(n, TOPK)
                    if k == 0:
                        cols = slice(n, n + TOPK)
                        act.wait_ge(sem["u_free"], t * SLOTS + UR + n + TOPK)
                        A(acts[:, cols], dots[:, cols], ACT.Gelu).then_inc(sem["gelu"], 1)
                        act.wait_ge(sem["coef"], t * PH + h + 1)
                    if n == 7 and not first:
                        final_root(t - 1)
                    if first and n in FIRST_EXP_AT:
                        exponentials(0, [FIRST_EXP_AT[n]])
                    if n >= 2 and not last:
                        ahead(t + 1, n - 2)
                    if not first or n >= DR:
                        act.wait_ge(sem["v_free"], t * SLOTS + n + 1 + VR - DR)
                    A(diag[:, n % DR, :], ident, ACT.Copy, scale=coef[:, n:n + 1]).then_inc(sem["diag"], 1)

            copy_mixed(0)
            for g, bank in enumerate(o_ps + s_ps):
                act.wait_ge(sem["skT_ps"], g + 1)
                A(skT[:, 4 * g:4 * g + 4, :], bank[:], ACT.Copy).then_inc(sem["skT"], 1)
            row_root(0)
            copy_rows(0)
            for g in range(4):
                copy_queries(0, g, first=True)
                copy_scores(0, g)
            exponentials(0, [0])
            tile(0, first=True)
            with act.Fori(1, TILES - 1) as t:
                tile(t)
            tile(TILES - 1, last=True)
            final_root(TILES - 1)

        @block.vector
        def _(dve):
            V = nc.vector

            def residual(T, half):
                hs = row(T)[:, BANK * half:BANK * (half + 1)]
                dve.wait_ge(sem["x_again"], 16 * (T + 1))
                dve.wait_ge(sem["out_ps"], 2 * T + 1 + half)
                V.tensor_tensor(hs, hs, q_ps[half][:], ALU.add).then_inc(sem["h"], 1)

            def normed(T):
                dve.wait_ge(sem["rms2"], T + 1)
                V.reciprocal(stat[:, 2:3], stat[:, 1:2]).then_inc(sem["rstd2"], 1)
                dve.wait_ge(sem["rstd2"], T + 1)
                V.scalar_tensor_tensor(xn_next[:], row(T), stat[:, 2:3], gain2[:], ALU.mult, ALU.mult).then_inc(sem["xn2"], 1)

            def route(T, part):
                step = Steps(sem["route"], ROUTE_STEPS, PARTS * T + part)
                sub = [s_buf[:, NK * n:NK * (n + 1)] for n in range(HC)]
                for g in range(4 // PARTS * part, 4 // PARTS * (part + 1)):
                    dve.wait_ge(sem["s"], 4 * T + g + 1)
                    dve.nop(nofuse=True)
                    four = range(4 * g, 4 * g + 4)
                    for half in range(2):
                        eight = slice(8 * half, 8 * half + 8)
                        for n in four:
                            last = V.max(top[:, n, eight], sub[n])
                        step.done(last)
                        yield
                        step.wait(dve)
                        for n in four:
                            last = V.max_index(topi[:, n, eight], top[:, n, eight], sub[n])
                        if half == 0:
                            step.done(last)
                            step.wait(dve)
                            for n in four:
                                last = V.match_replace(sub[n], top[:, n, eight], sub[n], LOWEST)
                        step.done(last)
                        yield
                        step.wait(dve)
                heads = range(HP * part, HP * (part + 1))
                slots = slice(PW * part, PW * (part + 1))
                pairs = slice(SIDES * HP * part, SIDES * HP * (part + 1))
                V.tensor_copy(topf[:, pairs, :], topi[:, pairs, :])
                t4 = top[:, pairs, :].rearrange("p (h c) k -> p h c k", c=SIDES)
                c4 = cand[:, 256 * HP * part:256 * HP * (part + 1)].rearrange("p (h a b) -> p h a b", a=TOPK, b=TOPK)
                step.done(V.tensor_tensor(c4, t4[:, :, 0, :].unsqueeze(3).to_broadcast([P, HP, TOPK, TOPK]),
                                          t4[:, :, 1, :].unsqueeze(2).to_broadcast([P, HP, TOPK, TOPK]), ALU.add))
                yield
                step.wait(dve)
                sums = [cand[:, 256 * h:256 * (h + 1)] for h in range(PH)]
                pos3 = pos[:].rearrange("p (h k) -> p h k", k=TOPK)
                for half in range(2):
                    eight = slice(8 * half, 8 * half + 8)
                    for h in heads:
                        last = V.max(best[:, h, eight], sums[h])
                    step.done(last)
                    yield
                    step.wait(dve)
                    for h in heads:
                        last = V.max_index(pos3[:, h, eight], best[:, h, eight], sums[h])
                    step.done(last)
                    if half == 0:
                        step.wait(dve)
                        for h in heads:
                            last = V.match_replace(sums[h], best[:, h, eight], sums[h], LOWEST)
                        step.done(last)
                    yield
                    step.wait(dve)
                exs, bests = (b[:, HP * part:HP * (part + 1), :] for b in (ex, best))
                V.tensor_tensor(exs, bests, bests[:, :, 0:1].to_broadcast([P, HP, TOPK]), ALU.subtract)\
                 .then_inc(sem["shifted"], 1)
                pos2, posf, key = (part_of_cand(part, i) for i in range(3))
                pos2 = pos2.bitcast(U32)
                V.tensor_scalar(pos2[:, 0:PW], pos[:, slots], 4, None, ALU.logical_shift_right)
                step.done(V.tensor_scalar(pos2[:, PW:2 * PW], pos[:, slots], 15, None, ALU.bitwise_and))
                step.wait(dve)
                step.done(V.tensor_copy(posf, pos2))
                step.wait(dve)
                yield
                iota = cst[:, C_IOTA:C_IOTA + TOPK].unsqueeze(1).to_broadcast([P, PW, TOPK])
                f4 = topf[:].rearrange("p (h c) k -> p h c k", c=SIDES)
                hot = s_buf[:, TOPK * PW * part:TOPK * PW * (part + 1)].rearrange("p (n a) -> p n a", a=TOPK)
                for c in range(SIDES):
                    place = posf[:, PW * c:PW * (c + 1)].unsqueeze(2).to_broadcast([P, PW, TOPK])
                    step.done(V.tensor_tensor(hot, place, iota, ALU.is_equal))
                    step.wait(dve)
                    for i, h in enumerate(heads):
                        hh = hot[:, TOPK * i:TOPK * (i + 1), :]
                        last = V.tensor_tensor(hh, hh, f4[:, h, c, :].unsqueeze(1).to_broadcast([P, TOPK, TOPK]), ALU.mult)
                    step.done(last)
                    yield
                    step.wait(dve)
                    step.done(V.tensor_reduce(key[:, PW * c:PW * (c + 1)], hot, AX.X, ALU.add))
                    yield
                    step.wait(dve)
                assert step.n == ROUTE_STEPS, step.n

            def publish(T, part, first=False):
                heads = slice(HP * part, HP * (part + 1))
                slots = slice(PW * part, PW * (part + 1))
                done = PARTS * T + part
                key = part_of_cand(part, 2)
                if not first:
                    dve.wait_ge(sem["staged"], PH * T)
                dve.wait_ge(sem["route"], ROUTE_STEPS * (done + 1))
                V.scalar_tensor_tensor(idx_next[:, slots], key[:, 0:PW], float(NK), key[:, PW:2 * PW], ALU.mult, ALU.add)\
                 .then_inc(sem["idx"], 1)
                dve.wait_ge(sem["ex"], T * PARTS + part + 1 if first else PARTS * (T + 1))
                V.tensor_reduce(soft[:, heads], ex[:, heads, :], AX.X, ALU.add).then_inc(sem["soft"], 1)
                dve.wait_ge(sem["soft"], 2 * done + 1)
                V.reciprocal(soft[:, 8 + HP * part:8 + HP * (part + 1)], soft[:, heads]).then_inc(sem["soft"], 1)
                dve.wait_ge(sem["soft"], 2 * done + 2)
                V.tensor_tensor(g_next[:, slots].rearrange("p (h k) -> p h k", k=TOPK), ex[:, heads, :],
                                soft[:, 8 + HP * part:8 + HP * (part + 1)].unsqueeze(2).to_broadcast([P, HP, TOPK]),
                                ALU.mult).then_inc(sem["g_next"], 1)

            def copy_weights(t, part):
                dve.wait_ge(sem["g_next"], PARTS * t + part + 1)
                slots = slice(PW * part, PW * (part + 1))
                V.tensor_copy(g_cur[:, slots], g_next[:, slots]).then_inc(sem["g_cur"], 1)

            def weigh(t, h):
                dve.wait_ge(sem["g_cur"], PARTS * t + h // HP + 1)
                cols = slice(TOPK * h, TOPK * (h + 1))
                dve.wait_ge(sem["gelu"], t * PH + h + 1)
                V.tensor_tensor(coef[:, cols], acts[:, cols], g_cur[:, cols], ALU.mult).then_inc(sem["coef"], 1)

            def add_residual(t):
                dve.wait_ge(sem["v_free"], (t + 1) * SLOTS + VR)
                for i in range(2):
                    hs = row(t)[:, BANK * i:BANK * (i + 1)]
                    V.tensor_tensor(hs, hs, o_ps[i][:], ALU.add).then_inc(sem["summed"], 1)

            def final_norm(t):
                dve.wait_ge(sem["rmsf"], t + 1)
                V.reciprocal(stat[:, 6:7], stat[:, 5:6]).then_inc(sem["rstdf"], 1)
                dve.wait_ge(sem["rstdf"], t + 1)
                V.scalar_tensor_tensor(row(t), row(t), stat[:, 6:7], gainf[:], ALU.mult, ALU.mult).then_inc(sem["y"], 1)

            def first_parts():
                for part in range(1, PARTS):
                    yield from route(0, part)
                    yield
                    publish(0, part, first=True)
                    copy_weights(0, part)

            def tile(t, first=False, last=False):
                if not first:
                    dve.wait_ge(sem["u_free"], UR + SLOTS * t)
                V.tensor_copy(xn_cur[:], xn_next[:]).then_inc(sem["cur"], 1)
                dve.wait_ge(sem["cur"], t + 1)
                early = first_parts() if first else None
                routing = None if last else chain.from_iterable(route(t + 1, part) for part in range(PARTS))
                for n in range(SLOTS):
                    h, k = divmod(n, TOPK)
                    dve.wait_ge(sem["u_in"][n % UR], 16 * (t * (SLOTS // UR) + n // UR + 1))
                    V.scalar_tensor_tensor(urow[:, n % UR, :], urow[:, n % UR, :], 1.0, xn_cur[:], ALU.mult, ALU.mult,
                                           accum_out=dots[:, n:n + 1]).then_inc(sem["u_free"], 1)
                    if k == 1 and h:
                        weigh(t, h - 1)
                    if n == 1:
                        if not first:
                            weigh(t - 1, PH - 1)
                            dve.wait_ge(sem["coef"], PH * t)
                        for part in range(1 if first else PARTS):
                            copy_weights(t, part)
                    if n == 16 and not first:
                        add_residual(t - 1)
                    if n in (27, 32) and not last:
                        residual(t + 1, int(n == 32))
                    if n == 38 and not last:
                        normed(t + 1)
                    if n == 25 and not first:
                        final_norm(t - 1)
                    if first and n in FIRST_SEARCH_AT:
                        next(early, None)
                    if not last and n in SEARCH_AT:
                        next(routing, None)
                    if not last and n == 119:
                        for _ in routing:
                            pass
                        for part in range(PARTS):
                            publish(t + 1, part)
                if last:
                    weigh(t, PH - 1)
                assert not first or next(early, None) is None

            V.memset(cred[:, 0:1], 0.0).then_inc(sem["u_free"], UR)
            V.memset(cred[:, 1:2], 0.0).then_inc(sem["v_free"], VR)
            dve.wait_ge(sem["gain2_in"], 16)
            residual(0, 0)
            residual(0, 1)
            normed(0)
            for _ in route(0, 0):
                pass
            publish(0, 0, first=True)
            dve.wait_ge(sem["gainf_in"], 16)
            tile(0, first=True)
            with dve.Fori(1, TILES - 1) as t:
                tile(t)
            tile(TILES - 1, last=True)
            add_residual(TILES - 1)
            final_norm(TILES - 1)


NAMES_MIX = """pad_zeroed x0_in gain1_in cst_in mix_in x1_in x_in rope_in gate_in hg_in xn S_new xT_ps xT decay_last
 ga_ps gate_g gqk_ps gaT z_ps gate_r rqk_ps gqk gv_ps log_a R_new cum_ps rope rv_ps gv gg_ps gqkk norm_g gT_ps norm_r
 rT_ps rv rg_ps gqs gT att_ps rT rqx kv_g_ps kv_r_ps att S_mid state0 o_ps o 
 ss rms absz decay sq_g centred sq_r hss hroot rstd roped kz hmean hrstd scaled mixed mixed_out""".split()
NAMES_PEER = """mixed_in x_again oT_ps oT out_ps h sk_in gain2_in gainf_in y stored idx staged u_free v_free xn2 x2T_ps x2T qT q_ps s s_ps diag summed skT_ps
 skT ss2 rms2 shifted ex ssf rmsf gelu coef rstd2 route soft g_next rstdf cur g_cur""".split()


def build(nc, io, out):
    with ExitStack() as ctx:
        sem = {n: ctx.enter_context(nc.semaphore(n)) for n in NAMES_MIX + NAMES_PEER}
        sem["w_in_in"] = [ctx.enter_context(nc.semaphore(f"w_in_in{i}")) for i in range(len(W_PARTS))]
        sem["w_out_in"] = [ctx.enter_context(nc.semaphore(f"w_out_in{i}")) for i in range(4)]
        sem["w_q_in"] = [ctx.enter_context(nc.semaphore(f"w_q_in{i}")) for i in range(4)]
        sem["u_in"] = [ctx.enter_context(nc.semaphore(f"u_in{i}")) for i in range(UR)]
        sem["v_in"] = [ctx.enter_context(nc.semaphore(f"v_in{i}")) for i in range(VR)]
        shared = {
            "mixed": nc.dram_tensor("mixed_dram", (TILES, P, D), F32).ap(),
            "cst": ctx.enter_context(nc.sbuf_tensor("cst_sb", [P, C_END], F32)),
        }
        with nc.Block() as block:
            mixer_phase(nc, block, io, shared, sem)
        with nc.Block() as block:
            peer_phase(nc, block, io, out, shared, sem)


def constants():
    import numpy as np
    f = np.float32
    c, m = np.zeros((P, C_END), f), np.zeros((P, M_END), f)
    rope = np.zeros((P, TILES + 1, ROPE_W), f)
    j, i = np.arange(P)[:, None], np.arange(P)[None, :]
    same = (j // CH) == (i // CH)
    c[:, C_ID:C_ID + P] = np.eye(P)
    m[:, M_TRI:M_TRI + P] = (same & (j <= i)) / 16.0
    m[:, M_REV:M_REV + P] = (same & (j > i)) / 16.0
    m[:, M_MASK:M_MASK + P] = same & (j <= i)
    m[:, M_IND:M_IND + 2] = (j // CH == np.arange(2)[None, :]) / 16.0
    c[:, C_ONE] = 1.0
    c[:, C_EPS] = EPS
    c[:, C_IOTA:C_IOTA + TOPK] = np.arange(TOPK)
    lg = np.log1p(-(2.0 ** (-5.0 - np.arange(HEADS))))
    scale = DK ** -0.5
    for h in range(HEADS):
        m[:, M_DMAT + P * h:M_DMAT + P * (h + 1)] = np.where(j <= i, np.exp(lg[h] * np.maximum(i - j, 0)), 0.0) * scale
        m[:, M_ZETA + h] = np.exp(lg[h] * (P - 1 - np.arange(P))) * scale
        rows = slice(DK * (h % 2), DK * (h % 2) + DK)
        m[rows, M_XI + P * (h // 2):M_XI + P * (h // 2 + 1)] = np.exp(lg[h] * (np.arange(P) + 1.0))[None, :]
        m[rows, M_GAM + h // 2] = np.exp(lg[h] * P)
    inv_freq = (f(10000.0) ** (-np.arange(0, DK, 2, dtype=f) / f(DK))).astype(f)
    for t in range(TILES + 1):
        pos = (np.arange(P) + P * t - (P - NMETA)).astype(f)
        ang = (pos[:, None] * inv_freq[None, :]).astype(f).astype(np.float64)
        rope[:, t, 0:32] = np.cos(ang)
        rope[:, t, 32:64] = -np.sin(ang)
        rope[:, t, 64:96] = np.sin(ang)
    return c, m, rope


_INS = ["x", "meta_tokens", "norm1_gain", "w_in", "gla_gate_w2", "gla_gate_b", "gla_norm_gain", "ret_norm_gain",
        "ret_norm_bias", "w_out", "norm2_gain", "peer_w_q", "peer_subkeys", "peer_u", "peer_v", "final_gain"]


def kernel(**inputs):
    import numpy as _np
    import concourse.bacc as _bacc
    from concourse import mybir as _mybir
    from concourse.bass_utils import run_bass_kernel_spmd as _run

    nc = _bacc.Bacc("TRN2", target_bir_lowering=False, num_devices=1)
    arrays, io = {}, {}
    for name in _INS:
        arrays[f"in_{name}"] = _np.ascontiguousarray(inputs[name])
    arrays["in_cst"], arrays["in_mix"], arrays["in_rope"] = constants()
    for name, a in arrays.items():
        io[name[3:]] = nc.dram_tensor(name, a.shape, _mybir.dt.from_np(a.dtype), kind="ExternalInput").ap()
    out = nc.dram_tensor("out_dram", (1, SEQ, D), _mybir.dt.float32, kind="ExternalOutput").ap()
    build(nc, io, out)
    r = _run(nc, [arrays], core_ids=[0])
    return r.results[0]["out_dram"]
```

```python
import concourse.bass as bass
from concourse import mybir
from contextlib import ExitStack
from itertools import chain

F32 = mybir.dt.float32
U32 = mybir.dt.uint32
ALU = mybir.AluOpType
ACT = mybir.ActivationFunctionType
AX = mybir.AxisListType

P = 128
D = 1024
KC = D // P
HEADS = 4
DK, DV = 64, 128
PAIRS = HEADS // 2
CH = 64
SEQ, NMETA = 1024, 16
TILES = SEQ // P
BANK = 512
EPS = 1e-6
GQK, GV, GG, GA, RQK, RV, RG = 0, 512, 1024, 1536, 1552, 2064, 2576
RANK = 16
IN_WIDTH = 3088
W_PARTS = [(GA, RV), (GQK, GV), (GV, GG), (RV, RG), (GG, GA), (RG, IN_WIDTH)]
PH, NK, TOPK = 8, 128, 16
SIDES = 2
HC = PH * SIDES
SLOTS = PH * TOPK
UR, VR, DR, HR = 4, 4, 8, 4
LOWEST = -3.4028235e38
C_ID, C_ONE, C_EPS, C_IOTA, C_END = 0, 128, 129, 130, 146
M_TRI, M_REV, M_MASK, M_DMAT, M_XI, M_ZETA, M_GAM, M_IND, M_END = 0, 128, 256, 384, 896, 1152, 1156, 1158, 1160
ROPE_W = 96


def mixer_phase(nc, block, io, shared, sem):
    cst = shared["cst"]
    ident = cst[:, C_ID:C_ID + P]
    with ExitStack() as ctx:
        def sb(name, shape, dt=F32):
            return ctx.enter_context(nc.sbuf_tensor(name, shape, dt))

        def ps(name):
            return ctx.enter_context(nc.psum_tensor(name, [P, BANK], F32))

        h_all = shared["tiles"]
        w_in = sb("w_in_sb", [P, KC, IN_WIDTH])
        mix = sb("mix_sb", [P, M_END])
        rope = sb("rope_sb", [P, TILES + 1, ROPE_W])
        gain1 = sb("gain1", [P, D])
        xn = sb("xn", [P, D])
        xT = sb("xT", [P, KC, P])
        junk = sb("junk", [P, D], mybir.dt.bfloat16)
        stat = sb("stat", [P, 4])
        gaT = sb("gaT", [RANK + 1, P])
        w2b = sb("w2b", [RANK + 1, HEADS * DK])
        absz = sb("absz", [P, 256])
        log_a = sb("log_a", [P, 256])
        decay = sb("decay", [P, 3, 256])
        a_last = sb("a_last", [P, PAIRS, 2])
        gqk = sb("gqk", [P, 512])
        gqkk = sb("gqkk", [P, 3, 256])
        gT = sb("gT", [P, PAIRS, P])
        gqs = sb("gqs", [P, PAIRS, 2, P])
        ropeA = sb("ropeA", [P, 512])
        rqk = sb("rqk", [P, 512])
        kz = sb("kz", [P, 256])
        rT = sb("rT", [P, 2 * PAIRS, P])
        rqx = sb("rqx", [P, PAIRS, P])
        att_g = sb("att_g", [P, HEADS, P])
        att_r = sb("att_r", [P, HEADS, P])
        v_g = sb("v_g", [P, 512])
        v_r = sb("v_r", [P, 512])
        gate = sb("gate", [P, D])
        S_prev = sb("S_prev", [P, PAIRS, 256])
        S_mid = sb("S_mid", [P, PAIRS, 256])
        R_prev = sb("R_prev", [P, PAIRS, 256])
        sq = sb("sq", [P, 512])
        sq2 = sb("sq2", [P, D])
        hstat = sb("hstat", [P, 32])
        hg = sb("hg", [P, 3, DV])

        o_sb = sb("o_sb", [P, 2, PAIRS, 2, DV])
        o_g = o_sb[:, 0].rearrange("p a e d -> p (a e d)")
        o_r = o_sb[:, 1].rearrange("p a e d -> p (a e d)")

        pa = shared["banks"] + [ps(f"pa{i}") for i in range(2, 8)]
        pT = [pa[2], pa[3]]


        @block.sync
        def _(sp):
            sp.wait_ge(sem["pad_zeroed"], 1)
            sp.dma_start(h_all[P - NMETA:P, 0, :], io["meta_tokens"][:, :]).then_inc(sem["x0_in"], 16)
            sp.dma_start(cst[:], io["cst"][:, :]).then_inc(sem["cst_in"], 16)
            sp.dma_start(gain1[:], io["norm1_gain"][0:1, :].to_broadcast([P, D])).then_inc(sem["gain1_in"], 16)

            def columns(i):
                start, end = W_PARTS[i]
                sp.dma_start(w_in[:, :, start:end], io["w_in"][0].rearrange("(k p) n -> p k n", p=P)[:, :, start:end])\
                    .then_inc(sem["w_in_in"][i], 16)

            columns(0)
            columns(1)
            sp.dma_start(w2b[0:RANK, :], io["gla_gate_w2"][0]).then_inc(sem["gate_in"], 16)
            sp.dma_start(w2b[RANK:RANK + 1, :], io["gla_gate_b"][:, :]).then_inc(sem["gate_in"], 16)
            sp.dma_start(mix[:], io["mix"][:, :]).then_inc(sem["mix_in"], 16)
            sp.dma_start(rope[:], io["rope"][:, :, :]).then_inc(sem["rope_in"], 16)
            columns(2)
            sp.dma_start(h_all[:, 1, :], io["x"][0, 0:P, :]).then_inc(sem["x1_in"], 16)
            for i in range(3, len(W_PARTS)):
                columns(i)
            sp.dma_start(h_all[:, 2:TILES + 1, :],
                         io["x"][0].rearrange("(t p) d -> p t d", p=P)[:, 1:TILES, :]).then_inc(sem["x_in"], 16)

            def store(t):
                sp.wait_ge(sem["mixed"], t)
                sp.dma_start(shared["mixed"].rearrange("t p d -> p t d")[:, bass.ds(t - 1, 1), :],
                             h_all[:, bass.ds(t, 1), :]).then_inc(sem["mixed_out"], 16)

            with sp.Fori(1, TILES) as t:
                store(t)
            sp.wait_ge(sem["mixed_out"], 16 * (TILES - 1))
            for i in range(4):
                sp.dma_start(h_all[:, 2 * i:2 * i + 2, :], io["w_out"][0].rearrange("(k p) n -> p k n", p=P)[:, 2 * i:2 * i + 2, :])\
                    .then_inc(sem["w_out_in"][i], 16)
            sp.wait_ge(sem["xT_ps"], 2 * (TILES + 1))
            sp.dma_start(xn[:], shared["mixed"][0]).then_inc(sem["mixed_in"], 16)
            store(TILES)
            sp.wait_ge(sem["mixed_out"], 16 * TILES)

        @block.gpsimd
        def _(pool):
            for i, n in enumerate(("gla_norm_gain", "ret_norm_gain", "ret_norm_bias")):
                pool.dma_start(hg[:, i, :], io[n][0:1, :].to_broadcast([P, DV])).then_inc(sem["hg_in"], 16)

        @block.tensor
        def _(pe):
            def landed(wanted, part):
                if wanted:
                    pe.wait_ge(sem["w_in_in"][part], 16)

            def project(bank, w, src, col, skip=0):
                for k in range(KC):
                    last = nc.tensor.matmul(bank[:, skip:BANK], src[:, k, :], w[:, k, col + skip:col + BANK],
                                            start=(k == 0), stop=(k == KC - 1))
                return last

            def transpose_rows(t, prev=True):
                pe.wait_ge(sem["xn"], t + 1)
                if prev:
                    pe.wait_ge(sem["S_new"], t - 1)
                for k in range(KC):
                    last = nc.tensor.transpose(pT[k // 4][:, P * (k % 4):P * (k % 4 + 1)],
                                               xn[:, P * k:P * (k + 1)], ident)
                    if k % 4 == 3:
                        last.then_inc(sem["xT_ps"], 1)

            def scores(t):
                pe.wait_ge(sem["gqs"], t)
                pe.wait_ge(sem["gT"], t)
                pe.wait_ge(sem["rT"], t)
                for h in range(HEADS):
                    rows = slice(DK * (h % 2), DK * (h % 2) + DK)
                    for c in range(2):
                        nc.tensor.matmul(pa[6 + h % 2][:, P * (h // 2) + CH * c:P * (h // 2) + CH * (c + 1)], gT[rows, h // 2, :],
                                         gqs[rows, h // 2, c, CH * c:CH * (c + 1)], start=True, stop=True)
                for h in range(HEADS):
                    rows = slice(DK * (h % 2), DK * (h % 2) + DK)
                    last = nc.tensor.matmul(pa[6 + h % 2][:, 256 + P * (h // 2):256 + P * (h // 2 + 1)], rT[rows, 2 + h // 2, :],
                                            rT[rows, h // 2, :], start=True, stop=True)
                    if h >= 2:
                        last.then_inc(sem["att_ps"], 1)

            def outputs(t):
                pe.wait_ge(sem["att"], t)
                pe.wait_ge(sem["rqx"], t)
                pe.wait_ge(sem["S_mid"], t + 1)
                for h in range(HEADS):
                    rows = slice(DK * (h % 2), DK * (h % 2) + DK)
                    vc = slice(P * (h % 2), P * (h % 2) + P)
                    o = pa[6 + h % 2][:, P * (h // 2):P * (h // 2 + 1)]
                    nc.tensor.matmul(o, att_g[:, h, :], v_g[:, P * h:P * (h + 1)], start=True, stop=False)
                    nc.tensor.matmul(o, gqs[rows, h // 2, 0, :], S_prev[rows, h // 2, vc], start=False, stop=False)
                    nc.tensor.matmul(o, gqs[rows, h // 2, 1, :], S_mid[rows, h // 2, vc], start=False, stop=True)
                for h in range(HEADS):
                    rows = slice(DK * (h % 2), DK * (h % 2) + DK)
                    vc = slice(P * (h % 2), P * (h % 2) + P)
                    o = pa[6 + h % 2][:, 256 + P * (h // 2):256 + P * (h // 2 + 1)]
                    nc.tensor.matmul(o, att_r[:, h, :], v_r[:, P * h:P * (h + 1)], start=True, stop=False)
                    last = nc.tensor.matmul(o, rqx[rows, h // 2, :], R_prev[rows, h // 2, vc], start=False, stop=True)
                    if h >= 2:
                        last.then_inc(sem["o_ps"], 1)

            def tile(t, meta=False, first=False, final=False):
                q = 256 if meta else 0
                if meta:
                    pe.wait_ge(sem["w_in_in"][0], 16)
                    pe.wait_ge(sem["xT"], 2)
                else:
                    pe.wait_ge(sem["decay_last"], t)
                for k in range(KC):
                    last = nc.tensor.matmul(pa[4][0:RANK, 0:P], w_in[:, k, GA:GA + RANK], xT[:, k, :],
                                            start=(k == 0), stop=(k == KC - 1))
                last.then_inc(sem["ga_ps"], 1)
                if not (meta or first):
                    pe.wait_ge(sem["gate_g"], t - 1)
                landed(meta, 1)
                project(pa[0], w_in, xT, GQK, skip=q).then_inc(sem["gqk_ps"], 1)
                pe.wait_ge(sem["gaT"], t + 1)
                if meta:
                    pe.wait_ge(sem["gate_in"], 32)
                nc.tensor.matmul(pa[4][:, P:P + 256], gaT[:, :], w2b[:, :], start=True, stop=True).then_inc(sem["z_ps"], 1)
                if not (meta or first):
                    pe.wait_ge(sem["gate_r"], t - 1)
                project(pa[1], w_in, xT, RQK, skip=q).then_inc(sem["rqk_ps"], 1)
                pe.wait_ge(sem["gqk"], t + 1)
                landed(meta, 2)
                project(pa[0], w_in, xT, GV).then_inc(sem["gv_ps"], 1)
                pe.wait_ge(sem["log_a"], t + 1)
                if meta:
                    pe.wait_ge(sem["mix_in"], 16)
                else:
                    pe.wait_ge(sem["R_new"], t)
                nc.tensor.matmul(pa[5][:, 0:256], mix[:, M_TRI:M_TRI + P], log_a[:], start=True, stop=True)
                nc.tensor.matmul(pa[5][:, 256:512], mix[:, M_REV:M_REV + P], log_a[:], start=True, stop=True)
                for p in range(PAIRS):
                    last = nc.tensor.matmul(pa[4][:, 384 + 2 * p:386 + 2 * p], log_a[:, P * p:P * (p + 1)],
                                            mix[:, M_IND:M_IND + 2], start=True, stop=True)
                last.then_inc(sem["cum_ps"], 1)
                pe.wait_ge(sem["rope"], t + 1)
                landed(meta, 3)
                project(pa[1], w_in, xT, RV).then_inc(sem["rv_ps"], 1)
                pe.wait_ge(sem["gv"], t + 1)
                if not meta:
                    landed(first, 4)
                    project(pa[0], w_in, xT, GG).then_inc(sem["gg_ps"], 1)
                pe.wait_ge(sem["gqkk"], t + 1)
                if not (meta or first):
                    pe.wait_ge(sem["o"], 2 * (t - 1))
                if not meta:
                    for i in range(4):
                        last = nc.tensor.transpose(pa[6][:, P * i:P * (i + 1)],
                                                   gqkk[:, i // 2, P * (i % 2):P * (i % 2 + 1)], ident)
                    last.then_inc(sem["gT_ps"], 1)
                    for i in range(4):
                        last = nc.tensor.transpose(pa[7][:, P * i:P * (i + 1)], rqk[:, P * i:P * (i + 1)], ident)
                    last.then_inc(sem["rT_ps"], 1)
                pe.wait_ge(sem["rv"], t + 1)
                if not meta:
                    landed(first, 5)
                    project(pa[1], w_in, xT, RG).then_inc(sem["rg_ps"], 1)
                if not final:
                    transpose_rows(t + 1, prev=not meta)
                if not meta:
                    scores(t)
                if not final:
                    pe.wait_ge(sem["xT"], 2 * t + 4)
                for c in range(2):
                    for p in range(PAIRS):
                        rows = slice(CH * c, CH * (c + 1))
                        last = nc.tensor.matmul(pT[c][:, 256 * p:256 * (p + 1)], gqkk[rows, 2, P * p:P * (p + 1)],
                                                v_g[rows, 256 * p:256 * (p + 1)], start=True, stop=True)
                    last.then_inc(sem["kv_g_ps"], 1)
                for p in range(PAIRS):
                    last = nc.tensor.matmul(pa[5][:, 256 * p:256 * (p + 1)], kz[:, P * p:P * (p + 1)],
                                            v_r[:, 256 * p:256 * (p + 1)], start=True, stop=True)
                last.then_inc(sem["kv_r_ps"], 1)
                if not meta:
                    outputs(t)

            pe.wait_ge(sem["cst_in"], 16)
            transpose_rows(0, prev=False)
            tile(0, meta=True)
            tile(1, first=True)
            with pe.Fori(2, TILES) as t:
                tile(t)
            tile(TILES, final=True)
            pe.wait_ge(sem["mixed_in"], 16)
            pe.wait_ge(sem["S_new"], TILES + 1)
            for k in range(KC):
                last = nc.tensor.transpose(pT[k // 4][:, P * (k % 4):P * (k % 4 + 1)], xn[:, P * k:P * (k + 1)], ident)
                if k % 4 == 3:
                    last.then_inc(sem["oT_ps"], 1)
            pe.wait_ge(sem["oT"], 2)
            pe.wait_ge(sem["gate_g"], TILES)
            pe.wait_ge(sem["gate_r"], TILES)
            for i in range(4):
                pe.wait_ge(sem["w_out_in"][i], 16)
            for half in range(2):
                for k in range(KC):
                    last = nc.tensor.matmul(pa[half][:], xT[:, k, :], h_all[:, k, BANK * half:BANK * (half + 1)],
                                            start=(k == 0), stop=(k == KC - 1))
                last.then_inc(sem["out_ps"], 1)

        @block.scalar
        def _(act):
            A = nc.scalar.activation

            def row_root(t):
                A(junk[:], h_all[:, bass.ds(t, 1), :], ACT.Square, accum_out=stat[:, 0:1]).then_inc(sem["ss"], 1)
                act.wait_ge(sem["ss"], t + 1)
                A(stat[:, 1:2], stat[:, 0:1], ACT.Sqrt, bias=cst[:, C_EPS:C_EPS + 1], scale=1.0 / D).then_inc(sem["rms"], 1)

            def copy_rows(t):
                for i in range(2):
                    act.wait_ge(sem["xT_ps"], 2 * t + i + 1)
                    A(xT[:, 4 * i:4 * i + 4, :], pT[i][:], ACT.Copy).then_inc(sem["xT"], 1)

            def tile(t, meta=False, first=False, final=False):
                q = 256 if meta else 0
                if not final:
                    row_root(t + 1)
                act.wait_ge(sem["ga_ps"], t + 1)
                A(gaT[0:RANK, :], pa[4][0:RANK, 0:P], ACT.Copy).then_inc(sem["gaT"], 1)
                act.wait_ge(sem["gqk_ps"], t + 1)
                A(gqk[:, q:], pa[0][:, q:], ACT.Copy).then_inc(sem["gqk"], 1)
                act.wait_ge(sem["z_ps"], t + 1)
                A(absz[:], pa[4][:, P:P + 256], ACT.Abs).then_inc(sem["absz"], 1)
                act.wait_ge(sem["absz"], 3 * t + 1)
                A(absz[:], absz[:], ACT.Exp, scale=-1.0).then_inc(sem["absz"], 1)
                act.wait_ge(sem["absz"], 3 * t + 2)
                A(absz[:], absz[:], ACT.Ln, bias=cst[:, C_ONE:C_ONE + 1]).then_inc(sem["absz"], 1)
                act.wait_ge(sem["gv_ps"], t + 1)
                A(v_g[:], pa[0][:], ACT.Copy).then_inc(sem["gv"], 1)
                act.wait_ge(sem["cum_ps"], t + 1)
                A(a_last[:], pa[4][:, 384:388], ACT.Exp).then_inc(sem["decay_last"], 1)
                A(decay[:, 0, :], pa[5][:, 0:256], ACT.Exp)
                A(decay[:, 1, :], pa[5][:, 0:256], ACT.Exp, scale=-1.0)
                A(decay[:, 2, :], pa[5][:, 256:512], ACT.Exp).then_inc(sem["decay"], 1)
                act.wait_ge(sem["rv_ps"], t + 1)
                A(v_r[:], pa[1][:], ACT.Copy).then_inc(sem["rv"], 1)
                if not meta:
                    act.wait_ge(sem["gg_ps"], t)
                    A(gate[:, 0:512], pa[0][:], ACT.Silu).then_inc(sem["gate_g"], 1)
                    act.wait_ge(sem["gqs"], t)
                    A(gT[:], pa[6][:, 256:512], ACT.Copy).then_inc(sem["gT"], 1)
                    act.wait_ge(sem["rT_ps"], t)
                    A(rT[:], pa[7][:], ACT.Copy).then_inc(sem["rT"], 1)
                    act.wait_ge(sem["rg_ps"], t)
                    A(gate[:, 512:1024], pa[1][:], ACT.Silu).then_inc(sem["gate_r"], 1)
                if not final:
                    copy_rows(t + 1)
                if not meta:
                    for e in range(2):
                        act.wait_ge(sem["o_ps"], 2 * t + e - 1)
                        A(o_sb[:, :, :, e, :], pa[6 + e][:].rearrange("p (g a d) -> p g a d", g=2, a=PAIRS), ACT.Copy).then_inc(sem["o"], 1)
                    act.wait_ge(sem["o"], 2 * t)
                    A(sq[:], o_g, ACT.Square).then_inc(sem["sq_g"], 1)
                    if final:
                        for i in range(2):
                            act.wait_ge(sem["oT_ps"], i + 1)
                            A(xT[:, 4 * i:4 * i + 4, :], pT[i][:], ACT.Copy).then_inc(sem["oT"], 1)
                    act.wait_ge(sem["centred"], t)
                    A(sq2[:, 512:1024], sq2[:, 0:512], ACT.Square).then_inc(sem["sq_r"], 1)
                    act.wait_ge(sem["hss"], t)
                    A(hstat[:, 8:16], hstat[:, 0:8], ACT.Sqrt, bias=cst[:, C_EPS:C_EPS + 1], scale=1.0 / DV).then_inc(sem["hroot"], 1)

            act.wait_ge(sem["cst_in"], 16)
            act.wait_ge(sem["x0_in"], 16)
            row_root(0)
            copy_rows(0)
            act.wait_ge(sem["x1_in"], 16)
            tile(0, meta=True)
            act.wait_ge(sem["x_in"], 16)
            tile(1, first=True)
            with act.Fori(2, TILES) as t:
                tile(t)
            tile(TILES, final=True)

        @block.vector
        def _(dve):
            V = nc.vector

            def heads(ap, n=DV):
                return ap.rearrange("p (h d) -> p h d", d=n)

            def normed(t, prev=True):
                dve.wait_ge(sem["rms"], t + 1)
                V.reciprocal(stat[:, 2:3], stat[:, 1:2]).then_inc(sem["rstd"], 1)
                dve.wait_ge(sem["rstd"], t + 1)
                if prev:
                    dve.wait_ge(sem["xT_ps"], 2 * t)
                V.scalar_tensor_tensor(xn[:], h_all[:, bass.ds(t, 1), :].rearrange("p o d -> p (o d)"), stat[:, 2:3],
                                       gain1[:], ALU.mult, ALU.mult).then_inc(sem["xn"], 1)

            def finish(t):
                dve.wait_ge(sem["o"], 2 * t)
                V.tensor_reduce(hstat[:, 24:28], heads(o_r), AX.X, ALU.add).then_inc(sem["hmean"], 1)
                dve.wait_ge(sem["hmean"], 2 * t - 1)
                V.tensor_scalar(hstat[:, 28:32], hstat[:, 24:28], 1.0 / DV, None, ALU.mult).then_inc(sem["hmean"], 1)
                dve.wait_ge(sem["hmean"], 2 * t)
                V.tensor_tensor(heads(sq2[:, 0:512]), heads(o_r),
                                hstat[:, 28:32].unsqueeze(2).to_broadcast([P, HEADS, DV]), ALU.subtract).then_inc(sem["centred"], 1)
                dve.wait_ge(sem["sq_g"], t)
                V.tensor_reduce(hstat[:, 0:4], heads(sq[:]), AX.X, ALU.add)
                dve.wait_ge(sem["sq_r"], t)
                V.tensor_reduce(hstat[:, 4:8], heads(sq2[:, 512:1024]), AX.X, ALU.add).then_inc(sem["hss"], 1)
                dve.wait_ge(sem["hroot"], t)
                V.reciprocal(hstat[:, 16:24], hstat[:, 8:16]).then_inc(sem["hrstd"], 1)
                dve.wait_ge(sem["hrstd"], t)
                mixed = h_all[:, bass.ds(t, 1), :].rearrange("p o d -> p (o d)")
                rs = hstat[:, 16:24].unsqueeze(2)
                V.tensor_tensor(heads(mixed[:, 0:512]), heads(o_g), rs[:, 0:4, :].to_broadcast([P, HEADS, DV]), ALU.mult)
                V.tensor_tensor(heads(mixed[:, 512:1024]), heads(sq2[:, 0:512]), rs[:, 4:8, :].to_broadcast([P, HEADS, DV]), ALU.mult)\
                 .then_inc(sem["norm_r"], 1)
                dve.wait_ge(sem["norm_r"], t)
                V.tensor_tensor(heads(mixed[:, 0:512]), heads(mixed[:, 0:512]), hg[:, 0:1, :].to_broadcast([P, HEADS, DV]), ALU.mult)
                V.tensor_tensor(heads(mixed[:, 512:1024]), heads(mixed[:, 512:1024]), hg[:, 1:2, :].to_broadcast([P, HEADS, DV]), ALU.mult)\
                 .then_inc(sem["scaled"], 1)
                dve.wait_ge(sem["scaled"], 2 * t - 1)
                V.tensor_tensor(heads(mixed[:, 512:1024]), heads(mixed[:, 512:1024]), hg[:, 2:3, :].to_broadcast([P, HEADS, DV]), ALU.add)\
                 .then_inc(sem["scaled"], 1)
                dve.wait_ge(sem["scaled"], 2 * t)
                dve.wait_ge(sem["gate_r"], t)
                V.tensor_tensor(mixed, mixed, gate[:], ALU.mult).then_inc(sem["mixed"], 1)

            def tile(t, meta=False, first=False, final=False):
                dve.wait_ge(sem["absz"], 3 * t + 3)
                if not meta:
                    dve.wait_ge(sem["cum_ps"], t)
                V.scalar_tensor_tensor(log_a[:], pa[4][:, P:P + 256], 0.0, absz[:], ALU.min, ALU.subtract).then_inc(sem["log_a"], 1)
                dve.wait_ge(sem["rqk_ps"], t + 1)
                src = pa[1][:].rearrange("p (n s c) -> p n s c", s=2, c=DK // 2)
                tmp = ropeA[:].rearrange("p (n s c) -> p n s c", s=2, c=DK // 2)
                dst = rqk[:].rearrange("p (n s c) -> p n s c", s=2, c=DK // 2)
                rt = rope[:, bass.ds(t, 1), :]
                lo = HEADS if meta else 0
                cos = rt[:, :, 0:32].to_broadcast([P, 8 - lo, 32])
                for s in range(2):
                    V.tensor_tensor(dst[:, lo:, s, :], src[:, lo:, s, :], cos, ALU.mult)
                for s in range(2):
                    sin = rt[:, :, 32 + 32 * s:64 + 32 * s].to_broadcast([P, 8 - lo, 32])
                    last = V.tensor_tensor(tmp[:, lo:, s, :], src[:, lo:, 1 - s, :], sin, ALU.mult)
                last.then_inc(sem["rope"], 1)
                dve.wait_ge(sem["rope"], t + 1)
                V.tensor_tensor(rqk[:, DK * lo:], rqk[:, DK * lo:], ropeA[:, DK * lo:], ALU.add).then_inc(sem["roped"], 1)
                dve.wait_ge(sem["roped"], t + 1)
                zeta = mix[:, M_ZETA:M_ZETA + HEADS].unsqueeze(2).to_broadcast([P, HEADS, DK])
                V.tensor_tensor(heads(kz[:], DK), heads(rqk[:, 256:512], DK), zeta, ALU.mult)
                dve.wait_ge(sem["decay"], t + 1)
                dve.wait_ge(sem["gqk"], t + 1)
                if not meta:
                    V.scalar_tensor_tensor(gqkk[:, 0, :], gqk[:, 0:256], DK ** -0.5, decay[:, 0, :], ALU.mult, ALU.mult)
                    V.tensor_tensor(gqkk[:, 1, :], gqk[:, 256:512], decay[:, 1, :], ALU.mult)
                V.tensor_tensor(gqkk[:, 2, :], gqk[:, 256:512], decay[:, 2, :], ALU.mult).then_inc(sem["gqkk"], 1)
                if not final:
                    normed(t + 1)
                if not meta:
                    dve.wait_ge(sem["gT_ps"], t)
                    for c in range(2):
                        cs = slice(CH * c, CH * (c + 1))
                        last = V.tensor_copy(gqs[:, :, c, cs], pa[6][:, 0:256].rearrange("p (a i) -> p a i", i=P)[:, :, cs])
                    last.then_inc(sem["gqs"], 1)
                    dve.wait_ge(sem["rT"], t)
                    V.tensor_tensor(rqx[:], rT[:, 0:PAIRS, :],
                                    mix[:, M_XI:M_XI + 256].rearrange("p (a i) -> p a i", i=P), ALU.mult).then_inc(sem["rqx"], 1)
                    mask = mix[:, M_MASK:M_MASK + P].bitcast(U32).unsqueeze(1).to_broadcast([P, PAIRS, P])
                    dmat = mix[:, M_DMAT:M_DMAT + 512].rearrange("p (a e i) -> p a e i", e=2, i=P)
                    for e in range(2):
                        dve.wait_ge(sem["att_ps"], 2 * t + e - 1)
                        dve.nop(nofuse=True)
                        scores = pa[6 + e][:].rearrange("p (n i) -> p n i", i=P)
                        V.copy_predicated(att_g[:].rearrange("p (a e) i -> p a e i", e=2)[:, :, e, :], mask, scores[:, 0:2, :])
                        last = V.tensor_tensor(att_r[:].rearrange("p (a e) i -> p a e i", e=2)[:, :, e, :], scores[:, 2:4, :],
                                               dmat[:, :, e, :], ALU.mult)
                    last.then_inc(sem["att"], 1)
                dve.wait_ge(sem["kv_g_ps"], 2 * t + 1)
                dve.wait_ge(sem["decay_last"], t + 1)
                for p in range(PAIRS):
                    last = V.scalar_tensor_tensor(S_mid[:, p, :], S_prev[:, p, :], a_last[:, p, 0:1],
                                                  pT[0][:, 256 * p:256 * (p + 1)], ALU.mult, ALU.add)
                last.then_inc(sem["S_mid"], 1)
                if not meta:
                    dve.wait_ge(sem["o_ps"], 2 * t)
                dve.wait_ge(sem["kv_g_ps"], 2 * t + 2)
                dve.wait_ge(sem["S_mid"], t + 1)
                for p in range(PAIRS):
                    last = V.scalar_tensor_tensor(S_prev[:, p, :], S_mid[:, p, :], a_last[:, p, 1:2],
                                                  pT[1][:, 256 * p:256 * (p + 1)], ALU.mult, ALU.add)
                last.then_inc(sem["S_new"], 1)
                dve.wait_ge(sem["kv_r_ps"], t + 1)
                for p in range(PAIRS):
                    last = V.scalar_tensor_tensor(R_prev[:, p, :], R_prev[:, p, :], mix[:, M_GAM + p:M_GAM + p + 1],
                                                  pa[5][:, 256 * p:256 * (p + 1)], ALU.mult, ALU.add)
                last.then_inc(sem["R_new"], 1)
                if not meta:
                    finish(t)

            V.memset(h_all[:, 0, :], 0.0).then_inc(sem["pad_zeroed"], 1)
            V.memset(gaT[:], 1.0)
            V.memset(gqs[:], 0.0)
            V.memset(att_g[:], 0.0)
            V.memset(S_prev[:], 0.0)
            V.memset(R_prev[:], 0.0).then_inc(sem["state0"], 1)
            dve.wait_ge(sem["gain1_in"], 16)
            dve.wait_ge(sem["cst_in"], 16)
            dve.wait_ge(sem["state0"], 1)
            normed(0, prev=False)
            dve.wait_ge(sem["hg_in"], 48)
            dve.wait_ge(sem["mix_in"], 16)
            dve.wait_ge(sem["rope_in"], 16)
            tile(0, meta=True)
            tile(1, first=True)
            with dve.Fori(2, TILES) as t:
                tile(t)
            tile(TILES, final=True)


class Steps:

    def __init__(self, sem, per_tile, tile):
        self.sem, self.per_tile, self.base, self.n = sem, per_tile, tile * per_tile, 0

    def done(self, instruction):
        self.n += 1
        instruction.then_inc(self.sem, 1)

    def wait(self, engine):
        engine.wait_ge(self.sem, self.base + self.n)
        engine.nop(nofuse=True)


MIX_AT = 4
OUT_AT = {n: i for i, n in enumerate((6, 7, 8, 9, 11, 12, 13, 14))}
ROWS_AT = 23
QUERY_AT = {26 + 2 * n: n for n in range(HC)}
SCORE_AT = {35 + 8 * g: g for g in range(4)}
SEARCH_AT = range(55, 119)
EXP_AT = 93
FIRST_EXP_AT = {0: 1, 12: 2, 28: 3}
FIRST_SEARCH_AT = range(3, 52)
PARTS = 4
PW = SLOTS // PARTS
HP = PH // PARTS
ROUTE_STEPS = 20 // PARTS + 14


def peer_phase(nc, block, io, out, shared, sem):
    cst = shared["cst"]
    ident = cst[:, C_ID:C_ID + P]
    with ExitStack() as ctx:
        def sb(name, shape, dt=F32):
            return ctx.enter_context(nc.sbuf_tensor(name, shape, dt))

        def ps(name):
            return ctx.enter_context(nc.psum_tensor(name, [P, BANK], F32))

        w_q = sb("w_q", [P, KC, HC * P])
        skT = sb("skT", [P, HC, NK])
        w_out = shared["tiles"][:, 0:KC, :]
        h_ring = sb("h_ring", [P, HR, D])
        urow = sb("urow", [P, UR, D])
        s_buf = sb("s_buf", [P, HC * NK])
        cand = sb("cand", [P, PH * TOPK * TOPK])
        vrow = sb("vrow", [P, VR, D])
        diag = sb("diag", [P, DR, P])
        gain2 = sb("gain2", [P, D])
        gainf = shared["tiles"][:, KC, :]
        xn_next = sb("xn_next", [P, D])
        xn_cur = sb("xn_cur", [P, D])
        xT = sb("xT_b", [P, KC, P])
        top = sb("top", [P, HC, TOPK])
        topi = sb("topi", [P, HC, TOPK], U32)
        topf = sb("topf", [P, HC, TOPK])
        best = sb("best", [P, PH, TOPK])
        pos = sb("pos", [P, SLOTS], U32)
        idx_next = sb("idx_next", [P, SLOTS], U32)
        idx_cur = sb("idx_cur", [P, SLOTS], U32)
        ex = sb("ex", [P, PH, TOPK])
        soft = sb("soft", [P, 16])
        g_next = sb("g_next", [P, SLOTS])
        g_cur = sb("g_cur", [P, SLOTS])
        dots = sb("dots", [P, SLOTS])
        acts = sb("acts", [P, SLOTS])
        coef = sb("coef", [P, SLOTS])
        junk = sb("junk_b", [P, D], mybir.dt.bfloat16)
        cred = sb("cred", [P, 2])
        stat = sb("stat_b", [P, 8])

        qT = cand[:].rearrange("p (n i) -> p n i", i=P)

        def part_of_cand(part, i):
            start = HC * P // PARTS * part + SIDES * PW * i
            return cand[:, start:start + SIDES * PW]

        sk_raw = [urow[:, 0, :], urow[:, 1, :]]
        o_ps = [ps("o_ps0"), ps("o_ps1")]
        x_ps = [ps("x_ps0"), ps("x_ps1")]
        q_ps = shared["banks"]
        s_ps = [ps("s_ps0"), ps("s_ps1")]

        def row(t):
            return h_ring[:, bass.ds(t % HR, 1), :].rearrange("p o d -> p (o d)")

        @block.sync
        def _(sp):
            def load_mixed(t):
                sp.dma_start(xn_next[:].unsqueeze(1), shared["mixed"].rearrange("t p d -> p t d")[:, bass.ds(t, 1), :])\
                    .then_inc(sem["mixed_in"], 16)

            def load_x(t):
                sp.dma_start(h_ring[:, bass.ds(t % HR, 1), :], io["x"][0].rearrange("(t p) d -> p t d", p=P)[:, bass.ds(t, 1), :])\
                    .then_inc(sem["x_again"], 16)

            def store(t):
                sp.wait_ge(sem["y"], t + 1)
                sp.dma_start(out[0].rearrange("(t p) d -> p t d", p=P)[:, bass.ds(t, 1), :], h_ring[:, bass.ds(t % HR, 1), :])\
                    .then_inc(sem["stored"], 16)

            load_x(0)
            sp.dma_start(gain2[:], io["norm2_gain"][0:1, :].to_broadcast([P, D])).then_inc(sem["gain2_in"], 16)
            for g in range(4):
                cols = slice(BANK * g, BANK * (g + 1))
                sp.dma_start(w_q[:, :, cols], io["peer_w_q"][0].rearrange("(k p) n -> p k n", p=P)[:, :, cols])\
                    .then_inc(sem["w_q_in"][g], 16)
                if g == 0:
                    sp.dma_start(urow[:].rearrange("p r (n d) -> p (r n) d", d=P)[:, 0:HC, :],
                                 io["peer_subkeys"][0].rearrange("h c n d -> n (h c) d")).then_inc(sem["sk_in"], 16)
            sp.dma_start(gainf, io["final_gain"].rearrange("(a d) -> a d", a=1).to_broadcast([P, D])).then_inc(sem["gainf_in"], 16)
            for t in range(HR - 1):
                sp.wait_ge(sem["cur"], t + 1)
                load_mixed(t + 1)
                load_x(t + 1)
                if t:
                    store(t - 1)
            with sp.Fori(HR - 1, TILES - 1) as t:
                sp.wait_ge(sem["cur"], t + 1)
                load_mixed(t + 1)
                sp.wait_ge(sem["stored"], 16 * (t + 2 - HR))
                load_x(t + 1)
                store(t - 1)
            store(TILES - 2)
            store(TILES - 1)
            sp.wait_ge(sem["stored"], 16 * TILES)

        @block.gpsimd
        def _(pool):
            def gather(table, ring, n, size, free, landed, t):
                pool.wait_ge(free, t * SLOTS + n + 1)
                pool.nop(nofuse=True)
                pool.indirect_dma_start(out=ring[:, n % size, :], out_offset=None, in_=table,
                                        in_offset=bass.IndirectOffsetOnAxis(ap=idx_cur[:, n:n + 1], axis=0))\
                    .then_inc(landed[n % size], 16)

            def stage(t, h, count):
                cols = slice(TOPK * h, TOPK * (h + 1))
                pool.tensor_copy(idx_cur[:, cols], idx_next[:, cols]).then_inc(sem["staged"], 1)
                pool.wait_ge(sem["staged"], count + 1)

            def gather_u(t, n):
                gather(io["peer_u"][0], urow, n, UR, sem["u_free"], sem["u_in"], t)

            def tile(t, last=False):
                for h in range(PH):
                    ahead = (t, h + 1) if h < PH - 1 else (t + 1, 0)
                    if h == PH - 1 and not last:
                        pool.wait_ge(sem["idx"], PARTS * (t + 2))
                        pool.nop(nofuse=True)
                    if h < PH - 1 and (h + 1) % HP == 0:
                        pool.wait_ge(sem["idx"], PARTS * t + (h + 1) // HP + 1)
                        pool.nop(nofuse=True)
                    if not (h == PH - 1 and last):
                        stage(*ahead, PH * t + h + 1)
                    for k in range(TOPK):
                        if not (h == PH - 1 and last):
                            gather_u(ahead[0], TOPK * ahead[1] + k)
                        gather(io["peer_v"][0], vrow, TOPK * h + k, VR, sem["v_free"], sem["v_in"], t)

            pool.wait_ge(sem["idx"], 1)
            stage(0, 0, 0)
            for k in range(TOPK):
                gather_u(0, k)
            with pool.Fori(0, TILES - 1) as t:
                tile(t)
            tile(TILES - 1, last=True)

        @block.tensor
        def _(pe):
            def transpose_mixed(T):
                pe.wait_ge(sem["mixed_in"], 16 * (T + 1))
                for k in range(KC):
                    last = nc.tensor.transpose(x_ps[k // 4][:, P * (k % 4):P * (k % 4 + 1)],
                                               xn_next[:, P * k:P * (k + 1)], ident)
                    if k % 4 == 3:
                        last.then_inc(sem["oT_ps"], 1)

            def project_out(T, part):
                half, quarter = divmod(part, 4)
                if part == 0:
                    pe.wait_ge(sem["oT"], 2 * T + 2)
                for k in (2 * quarter, 2 * quarter + 1):
                    last = nc.tensor.matmul(q_ps[half][:], xT[:, k, :], w_out[:, k, BANK * half:BANK * (half + 1)],
                                            start=(k == 0), stop=(k == KC - 1))
                if quarter == 3:
                    last.then_inc(sem["out_ps"], 1)

            def transpose_rows(T):
                pe.wait_ge(sem["xn2"], T + 1)
                for k in range(KC):
                    last = nc.tensor.transpose(x_ps[k // 4][:, P * (k % 4):P * (k % 4 + 1)],
                                               xn_next[:, P * k:P * (k + 1)], ident)
                    if k % 4 == 3:
                        last.then_inc(sem["x2T_ps"], 1)

            def query(T, n):
                g = n // 4
                if n == 0:
                    pe.wait_ge(sem["x2T"], 2 * T + 2)
                if n % 4 == 0 and g >= 2:
                    pe.wait_ge(sem["qT"], 4 * T + g - 1)
                for k in range(KC):
                    last = nc.tensor.matmul(q_ps[g % 2][:, P * (n % 4):P * (n % 4 + 1)],
                                            w_q[:, k, P * n:P * (n + 1)], xT[:, k, :],
                                            start=(k == 0), stop=(k == KC - 1))
                if n % 4 == 3:
                    last.then_inc(sem["q_ps"], 1)

            def scores(T, g):
                pe.wait_ge(sem["qT"], 4 * T + g + 1)
                if g >= 2:
                    pe.wait_ge(sem["s"], 4 * T + g - 1)
                for n in range(4 * g, 4 * g + 4):
                    last = nc.tensor.matmul(s_ps[g % 2][:, P * (n % 4):P * (n % 4 + 1)],
                                            qT[:, n, :], skT[:, n, :], start=True, stop=True)
                last.then_inc(sem["s_ps"], 1)

            def ahead(T, n):
                if n == MIX_AT:
                    transpose_mixed(T)
                if n in OUT_AT:
                    project_out(T, OUT_AT[n])
                if n == ROWS_AT:
                    transpose_rows(T)
                if n in QUERY_AT:
                    query(T, QUERY_AT[n])
                if n in SCORE_AT:
                    scores(T, SCORE_AT[n])

            def transpose_subkeys():
                pe.wait_ge(sem["sk_in"], 16)
                for g, bank in enumerate(s_ps + o_ps):
                    for n in range(4):
                        last = nc.tensor.transpose(bank[:, P * n:P * (n + 1)],
                                                   sk_raw[g // 2][:, P * (4 * (g % 2) + n):P * (4 * (g % 2) + n + 1)], ident)
                    last.then_inc(sem["skT_ps"], 1)

            def tile(t, first=False, last=False):
                if not first:
                    pe.wait_ge(sem["summed"], 2 * t)
                for n in range(SLOTS):
                    if not last:
                        ahead(t + 1, n)
                    pe.wait_ge(sem["v_in"][n % VR], 16 * (t * (SLOTS // VR) + n // VR + 1))
                    pe.wait_ge(sem["diag"], t * SLOTS + n + 1)
                    for i in range(2):
                        product = nc.tensor.matmul(o_ps[i][:], diag[:, n % DR, :], vrow[:, n % VR, BANK * i:BANK * (i + 1)],
                                                   start=(n == 0), stop=(n == SLOTS - 1))
                    product.then_inc(sem["v_free"], 1)

            transpose_rows(0)
            for g in range(4):
                pe.wait_ge(sem["w_q_in"][g], 16)
                for n in range(4 * g, 4 * g + 4):
                    query(0, n)
                if g == 0:
                    transpose_subkeys()
                pe.wait_ge(sem["skT"], g + 1)
                scores(0, g)
            tile(0, first=True)
            with pe.Fori(1, TILES - 1) as t:
                tile(t)
            tile(TILES - 1, last=True)

        @block.scalar
        def _(act):
            A = nc.scalar.activation

            def row_root(T):
                act.wait_ge(sem["h"], 2 * T + 2)
                A(xT[:].rearrange("p k i -> p (k i)"), row(T), ACT.Square, accum_out=stat[:, 0:1]).then_inc(sem["ss2"], 1)
                act.wait_ge(sem["ss2"], T + 1)
                A(stat[:, 1:2], stat[:, 0:1], ACT.Sqrt, bias=cst[:, C_EPS:C_EPS + 1], scale=1.0 / D).then_inc(sem["rms2"], 1)

            def copy_mixed(T):
                for i in range(2):
                    act.wait_ge(sem["oT_ps"], 2 * T + i + 1)
                    A(xT[:, 4 * i:4 * i + 4, :], x_ps[i][:], ACT.Copy).then_inc(sem["oT"], 1)

            def copy_rows(T):
                for i in range(2):
                    act.wait_ge(sem["x2T_ps"], 2 * T + i + 1)
                    A(xT[:, 4 * i:4 * i + 4, :], x_ps[i][:], ACT.Copy).then_inc(sem["x2T"], 1)

            def copy_queries(T, g, first=False):
                act.wait_ge(sem["q_ps"], 4 * T + g + 1)
                if g == 0 and not first:
                    act.wait_ge(sem["idx"], PARTS * T)
                A(qT[:, 4 * g:4 * g + 4, :], q_ps[g % 2][:], ACT.Copy).then_inc(sem["qT"], 1)

            def copy_scores(T, g):
                act.wait_ge(sem["s_ps"], 4 * T + g + 1)
                A(s_buf[:, BANK * g:BANK * (g + 1)], s_ps[g % 2][:], ACT.Copy).then_inc(sem["s"], 1)

            def ahead(T, n):
                if n == MIX_AT:
                    copy_mixed(T)
                if n == ROWS_AT - 4:
                    row_root(T)
                if n == ROWS_AT:
                    copy_rows(T)
                if n in QUERY_AT and QUERY_AT[n] % 4 == 3:
                    copy_queries(T, QUERY_AT[n] // 4)
                if n in SCORE_AT:
                    copy_scores(T, SCORE_AT[n])
                if n == EXP_AT:
                    exponentials(T)

            def exponentials(T, parts=range(PARTS)):
                heads = slice(HP * parts[0], HP * (parts[-1] + 1))
                act.wait_ge(sem["shifted"], PARTS * T + parts[-1] + 1)
                A(ex[:, heads, :], ex[:, heads, :], ACT.Exp).then_inc(sem["ex"], len(parts))

            def final_root(t):
                act.wait_ge(sem["summed"], 2 * t + 2)
                A(junk[:], row(t), ACT.Square, accum_out=stat[:, 4:5]).then_inc(sem["ssf"], 1)
                act.wait_ge(sem["ssf"], t + 1)
                A(stat[:, 5:6], stat[:, 4:5], ACT.Sqrt, bias=cst[:, C_EPS:C_EPS + 1], scale=1.0 / D).then_inc(sem["rmsf"], 1)

            def tile(t, first=False, last=False):
                for n in range(SLOTS):
                    h, k = divmod(n, TOPK)
                    if k == 0:
                        cols = slice(n, n + TOPK)
                        act.wait_ge(sem["u_free"], t * SLOTS + UR + n + TOPK)
                        A(acts[:, cols], dots[:, cols], ACT.Gelu).then_inc(sem["gelu"], 1)
                        act.wait_ge(sem["coef"], t * PH + h + 1)
                    if n == 7 and not first:
                        final_root(t - 1)
                    if first and n in FIRST_EXP_AT:
                        exponentials(0, [FIRST_EXP_AT[n]])
                    if n >= 2 and not last:
                        ahead(t + 1, n - 2)
                    if not first or n >= DR:
                        act.wait_ge(sem["v_free"], t * SLOTS + n + 1 + VR - DR)
                    A(diag[:, n % DR, :], ident, ACT.Copy, scale=coef[:, n:n + 1]).then_inc(sem["diag"], 1)

            row_root(0)
            copy_rows(0)
            for g in range(4):
                copy_queries(0, g, first=True)
                for i in {0: (0, 1), 1: (2, 3)}.get(g, ()):
                    act.wait_ge(sem["skT_ps"], i + 1)
                    A(skT[:, 4 * i:4 * i + 4, :], (s_ps + o_ps)[i][:], ACT.Copy).then_inc(sem["skT"], 1)
                copy_scores(0, g)
            exponentials(0, [0])
            tile(0, first=True)
            with act.Fori(1, TILES - 1) as t:
                tile(t)
            tile(TILES - 1, last=True)
            final_root(TILES - 1)

        @block.vector
        def _(dve):
            V = nc.vector

            def residual(T, half):
                hs = row(T)[:, BANK * half:BANK * (half + 1)]
                dve.wait_ge(sem["x_again"], 16 * (T + 1))
                dve.wait_ge(sem["out_ps"], 2 * T + 1 + half)
                V.tensor_tensor(hs, hs, q_ps[half][:], ALU.add).then_inc(sem["h"], 1)

            def normed(T):
                dve.wait_ge(sem["rms2"], T + 1)
                V.reciprocal(stat[:, 2:3], stat[:, 1:2]).then_inc(sem["rstd2"], 1)
                dve.wait_ge(sem["rstd2"], T + 1)
                V.scalar_tensor_tensor(xn_next[:], row(T), stat[:, 2:3], gain2[:], ALU.mult, ALU.mult).then_inc(sem["xn2"], 1)

            def route(T, part):
                step = Steps(sem["route"], ROUTE_STEPS, PARTS * T + part)
                sub = [s_buf[:, NK * n:NK * (n + 1)] for n in range(HC)]
                for g in range(4 // PARTS * part, 4 // PARTS * (part + 1)):
                    dve.wait_ge(sem["s"], 4 * T + g + 1)
                    dve.nop(nofuse=True)
                    four = range(4 * g, 4 * g + 4)
                    for half in range(2):
                        eight = slice(8 * half, 8 * half + 8)
                        for n in four:
                            last = V.max(top[:, n, eight], sub[n])
                        step.done(last)
                        yield
                        step.wait(dve)
                        for n in four:
                            last = V.max_index(topi[:, n, eight], top[:, n, eight], sub[n])
                        if half == 0:
                            step.done(last)
                            step.wait(dve)
                            for n in four:
                                last = V.match_replace(sub[n], top[:, n, eight], sub[n], LOWEST)
                        step.done(last)
                        yield
                        step.wait(dve)
                heads = range(HP * part, HP * (part + 1))
                slots = slice(PW * part, PW * (part + 1))
                pairs = slice(SIDES * HP * part, SIDES * HP * (part + 1))
                V.tensor_copy(topf[:, pairs, :], topi[:, pairs, :])
                t4 = top[:, pairs, :].rearrange("p (h c) k -> p h c k", c=SIDES)
                c4 = cand[:, 256 * HP * part:256 * HP * (part + 1)].rearrange("p (h a b) -> p h a b", a=TOPK, b=TOPK)
                step.done(V.tensor_tensor(c4, t4[:, :, 0, :].unsqueeze(3).to_broadcast([P, HP, TOPK, TOPK]),
                                          t4[:, :, 1, :].unsqueeze(2).to_broadcast([P, HP, TOPK, TOPK]), ALU.add))
                yield
                step.wait(dve)
                sums = [cand[:, 256 * h:256 * (h + 1)] for h in range(PH)]
                pos3 = pos[:].rearrange("p (h k) -> p h k", k=TOPK)
                for half in range(2):
                    eight = slice(8 * half, 8 * half + 8)
                    for h in heads:
                        last = V.max(best[:, h, eight], sums[h])
                    step.done(last)
                    yield
                    step.wait(dve)
                    for h in heads:
                        last = V.max_index(pos3[:, h, eight], best[:, h, eight], sums[h])
                    step.done(last)
                    if half == 0:
                        step.wait(dve)
                        for h in heads:
                            last = V.match_replace(sums[h], best[:, h, eight], sums[h], LOWEST)
                        step.done(last)
                    yield
                    step.wait(dve)
                exs, bests = (b[:, HP * part:HP * (part + 1), :] for b in (ex, best))
                V.tensor_tensor(exs, bests, bests[:, :, 0:1].to_broadcast([P, HP, TOPK]), ALU.subtract)\
                 .then_inc(sem["shifted"], 1)
                pos2, posf, key = (part_of_cand(part, i) for i in range(3))
                pos2 = pos2.bitcast(U32)
                V.tensor_scalar(pos2[:, 0:PW], pos[:, slots], 4, None, ALU.logical_shift_right)
                step.done(V.tensor_scalar(pos2[:, PW:2 * PW], pos[:, slots], 15, None, ALU.bitwise_and))
                step.wait(dve)
                step.done(V.tensor_copy(posf, pos2))
                step.wait(dve)
                yield
                iota = cst[:, C_IOTA:C_IOTA + TOPK].unsqueeze(1).to_broadcast([P, PW, TOPK])
                f4 = topf[:].rearrange("p (h c) k -> p h c k", c=SIDES)
                hot = s_buf[:, TOPK * PW * part:TOPK * PW * (part + 1)].rearrange("p (n a) -> p n a", a=TOPK)
                for c in range(SIDES):
                    place = posf[:, PW * c:PW * (c + 1)].unsqueeze(2).to_broadcast([P, PW, TOPK])
                    step.done(V.tensor_tensor(hot, place, iota, ALU.is_equal))
                    step.wait(dve)
                    for i, h in enumerate(heads):
                        hh = hot[:, TOPK * i:TOPK * (i + 1), :]
                        last = V.tensor_tensor(hh, hh, f4[:, h, c, :].unsqueeze(1).to_broadcast([P, TOPK, TOPK]), ALU.mult)
                    step.done(last)
                    yield
                    step.wait(dve)
                    step.done(V.tensor_reduce(key[:, PW * c:PW * (c + 1)], hot, AX.X, ALU.add))
                    yield
                    step.wait(dve)
                assert step.n == ROUTE_STEPS, step.n

            def publish(T, part, first=False):
                heads = slice(HP * part, HP * (part + 1))
                slots = slice(PW * part, PW * (part + 1))
                done = PARTS * T + part
                key = part_of_cand(part, 2)
                if not first:
                    dve.wait_ge(sem["staged"], PH * T)
                dve.wait_ge(sem["route"], ROUTE_STEPS * (done + 1))
                V.scalar_tensor_tensor(idx_next[:, slots], key[:, 0:PW], float(NK), key[:, PW:2 * PW], ALU.mult, ALU.add)\
                 .then_inc(sem["idx"], 1)
                dve.wait_ge(sem["ex"], T * PARTS + part + 1 if first else PARTS * (T + 1))
                V.tensor_reduce(soft[:, heads], ex[:, heads, :], AX.X, ALU.add).then_inc(sem["soft"], 1)
                dve.wait_ge(sem["soft"], 2 * done + 1)
                V.reciprocal(soft[:, 8 + HP * part:8 + HP * (part + 1)], soft[:, heads]).then_inc(sem["soft"], 1)
                dve.wait_ge(sem["soft"], 2 * done + 2)
                V.tensor_tensor(g_next[:, slots].rearrange("p (h k) -> p h k", k=TOPK), ex[:, heads, :],
                                soft[:, 8 + HP * part:8 + HP * (part + 1)].unsqueeze(2).to_broadcast([P, HP, TOPK]),
                                ALU.mult).then_inc(sem["g_next"], 1)

            def copy_weights(t, part):
                dve.wait_ge(sem["g_next"], PARTS * t + part + 1)
                slots = slice(PW * part, PW * (part + 1))
                V.tensor_copy(g_cur[:, slots], g_next[:, slots]).then_inc(sem["g_cur"], 1)

            def weigh(t, h):
                dve.wait_ge(sem["g_cur"], PARTS * t + h // HP + 1)
                cols = slice(TOPK * h, TOPK * (h + 1))
                dve.wait_ge(sem["gelu"], t * PH + h + 1)
                V.tensor_tensor(coef[:, cols], acts[:, cols], g_cur[:, cols], ALU.mult).then_inc(sem["coef"], 1)

            def add_residual(t):
                dve.wait_ge(sem["v_free"], (t + 1) * SLOTS + VR)
                for i in range(2):
                    hs = row(t)[:, BANK * i:BANK * (i + 1)]
                    V.tensor_tensor(hs, hs, o_ps[i][:], ALU.add).then_inc(sem["summed"], 1)

            def final_norm(t):
                dve.wait_ge(sem["rmsf"], t + 1)
                V.reciprocal(stat[:, 6:7], stat[:, 5:6]).then_inc(sem["rstdf"], 1)
                dve.wait_ge(sem["rstdf"], t + 1)
                V.scalar_tensor_tensor(row(t), row(t), stat[:, 6:7], gainf, ALU.mult, ALU.mult).then_inc(sem["y"], 1)

            def first_parts():
                for part in range(1, PARTS):
                    yield from route(0, part)
                    yield
                    publish(0, part, first=True)
                    copy_weights(0, part)

            def tile(t, first=False, last=False):
                if not first:
                    dve.wait_ge(sem["u_free"], UR + SLOTS * t)
                V.tensor_copy(xn_cur[:], xn_next[:]).then_inc(sem["cur"], 1)
                dve.wait_ge(sem["cur"], t + 1)
                early = first_parts() if first else None
                routing = None if last else chain.from_iterable(route(t + 1, part) for part in range(PARTS))
                for n in range(SLOTS):
                    h, k = divmod(n, TOPK)
                    dve.wait_ge(sem["u_in"][n % UR], 16 * (t * (SLOTS // UR) + n // UR + 1))
                    V.scalar_tensor_tensor(urow[:, n % UR, :], urow[:, n % UR, :], 1.0, xn_cur[:], ALU.mult, ALU.mult,
                                           accum_out=dots[:, n:n + 1]).then_inc(sem["u_free"], 1)
                    if k == 1 and h:
                        weigh(t, h - 1)
                    if n == 1:
                        if not first:
                            weigh(t - 1, PH - 1)
                            dve.wait_ge(sem["coef"], PH * t)
                        for part in range(1 if first else PARTS):
                            copy_weights(t, part)
                    if n == 16 and not first:
                        add_residual(t - 1)
                    if n in (27, 32) and not last:
                        residual(t + 1, int(n == 32))
                    if n == 38 and not last:
                        normed(t + 1)
                    if n == 25 and not first:
                        final_norm(t - 1)
                    if first and n in FIRST_SEARCH_AT:
                        next(early, None)
                    if not last and n in SEARCH_AT:
                        next(routing, None)
                    if not last and n == 119:
                        for _ in routing:
                            pass
                        for part in range(PARTS):
                            publish(t + 1, part)
                if last:
                    weigh(t, PH - 1)
                assert not first or next(early, None) is None

            V.memset(cred[:, 0:1], 0.0).then_inc(sem["u_free"], UR)
            V.memset(cred[:, 1:2], 0.0).then_inc(sem["v_free"], VR)
            dve.wait_ge(sem["gain2_in"], 16)
            residual(0, 0)
            residual(0, 1)
            normed(0)
            for _ in route(0, 0):
                pass
            publish(0, 0, first=True)
            dve.wait_ge(sem["gainf_in"], 16)
            tile(0, first=True)
            with dve.Fori(1, TILES - 1) as t:
                tile(t)
            tile(TILES - 1, last=True)
            add_residual(TILES - 1)
            final_norm(TILES - 1)


NAMES_MIX = """pad_zeroed x0_in gain1_in cst_in mix_in x1_in x_in rope_in gate_in hg_in xn S_new xT_ps xT decay_last
 ga_ps gate_g gqk_ps gaT z_ps gate_r rqk_ps gqk gv_ps log_a R_new cum_ps rope rv_ps gv gg_ps gqkk gT_ps norm_r
 rT_ps rv rg_ps gqs gT att_ps rT rqx kv_g_ps kv_r_ps att S_mid state0 o_ps o 
 ss rms absz decay sq_g centred sq_r hss hroot rstd roped hmean hrstd scaled mixed mixed_out""".split()
NAMES_PEER = """mixed_in x_again oT_ps oT out_ps h sk_in gain2_in gainf_in y stored idx staged u_free v_free xn2 x2T_ps x2T qT q_ps s s_ps diag summed skT_ps
 skT ss2 rms2 shifted ex ssf rmsf gelu coef rstd2 route soft g_next rstdf cur g_cur""".split()


def build(nc, io, out):
    with ExitStack() as ctx:
        sem = {n: ctx.enter_context(nc.semaphore(n)) for n in NAMES_MIX + NAMES_PEER}
        sem["w_in_in"] = [ctx.enter_context(nc.semaphore(f"w_in_in{i}")) for i in range(len(W_PARTS))]
        sem["w_out_in"] = [ctx.enter_context(nc.semaphore(f"w_out_in{i}")) for i in range(4)]
        sem["w_q_in"] = [ctx.enter_context(nc.semaphore(f"w_q_in{i}")) for i in range(4)]
        sem["u_in"] = [ctx.enter_context(nc.semaphore(f"u_in{i}")) for i in range(UR)]
        sem["v_in"] = [ctx.enter_context(nc.semaphore(f"v_in{i}")) for i in range(VR)]
        shared = {
            "mixed": nc.dram_tensor("mixed_dram", (TILES, P, D), F32).ap(),
            "tiles": ctx.enter_context(nc.sbuf_tensor("tiles", [P, TILES + 1, D], F32)),
            "banks": [ctx.enter_context(nc.psum_tensor(f"bank{i}", [P, BANK], F32)) for i in range(2)],
            "cst": ctx.enter_context(nc.sbuf_tensor("cst_sb", [P, C_END], F32)),
        }
        with nc.Block() as block:
            mixer_phase(nc, block, io, shared, sem)
        with nc.Block() as block:
            peer_phase(nc, block, io, out, shared, sem)


def constants():
    import numpy as np
    f = np.float32
    c, m = np.zeros((P, C_END), f), np.zeros((P, M_END), f)
    rope = np.zeros((P, TILES + 1, ROPE_W), f)
    j, i = np.arange(P)[:, None], np.arange(P)[None, :]
    same = (j // CH) == (i // CH)
    c[:, C_ID:C_ID + P] = np.eye(P)
    m[:, M_TRI:M_TRI + P] = (same & (j <= i)) / 16.0
    m[:, M_REV:M_REV + P] = (same & (j > i)) / 16.0
    m[:, M_MASK:M_MASK + P] = same & (j <= i)
    m[:, M_IND:M_IND + 2] = (j // CH == np.arange(2)[None, :]) / 16.0
    c[:, C_ONE] = 1.0
    c[:, C_EPS] = EPS
    c[:, C_IOTA:C_IOTA + TOPK] = np.arange(TOPK)
    lg = np.log1p(-(2.0 ** (-5.0 - np.arange(HEADS))))
    scale = DK ** -0.5
    for h in range(HEADS):
        m[:, M_DMAT + P * h:M_DMAT + P * (h + 1)] = np.where(j <= i, np.exp(lg[h] * np.maximum(i - j, 0)), 0.0) * scale
        m[:, M_ZETA + h] = np.exp(lg[h] * (P - 1 - np.arange(P))) * scale
        rows = slice(DK * (h % 2), DK * (h % 2) + DK)
        m[rows, M_XI + P * (h // 2):M_XI + P * (h // 2 + 1)] = np.exp(lg[h] * (np.arange(P) + 1.0))[None, :]
        m[rows, M_GAM + h // 2] = np.exp(lg[h] * P)
    inv_freq = (f(10000.0) ** (-np.arange(0, DK, 2, dtype=f) / f(DK))).astype(f)
    for t in range(TILES + 1):
        pos = (np.arange(P) + P * t - (P - NMETA)).astype(f)
        ang = (pos[:, None] * inv_freq[None, :]).astype(f).astype(np.float64)
        rope[:, t, 0:32] = np.cos(ang)
        rope[:, t, 32:64] = -np.sin(ang)
        rope[:, t, 64:96] = np.sin(ang)
    return c, m, rope


_INS = ["x", "meta_tokens", "norm1_gain", "w_in", "gla_gate_w2", "gla_gate_b", "gla_norm_gain", "ret_norm_gain",
        "ret_norm_bias", "w_out", "norm2_gain", "peer_w_q", "peer_subkeys", "peer_u", "peer_v", "final_gain"]


def kernel(**inputs):
    import numpy as _np
    import concourse.bacc as _bacc
    from concourse import mybir as _mybir
    from concourse.bass_utils import run_bass_kernel_spmd as _run

    nc = _bacc.Bacc("TRN2", target_bir_lowering=False, num_devices=1)
    arrays, io = {}, {}
    for name in _INS:
        arrays[f"in_{name}"] = _np.ascontiguousarray(inputs[name])
    arrays["in_cst"], arrays["in_mix"], arrays["in_rope"] = constants()
    for name, a in arrays.items():
        io[name[3:]] = nc.dram_tensor(name, a.shape, _mybir.dt.from_np(a.dtype), kind="ExternalInput").ap()
    out = nc.dram_tensor("out_dram", (1, SEQ, D), _mybir.dt.float32, kind="ExternalOutput").ap()
    build(nc, io, out)
    r = _run(nc, [arrays], core_ids=[0])
    return r.results[0]["out_dram"]
```
